# Optimizing a Trainium2 kernel written in Bass

```python
import math
import jax, jax.numpy as jnp
from jax import lax
import numpy as np

D_MODEL = 2048
BATCH = 1
SEQ = 256
DEPTH = 1
DEC_BATCH = 8
DEC_SEQ = 8
PAST_LEN = 2048
PAGE_SIZE = 128

SSM_EXPAND = 2
D_INNER = SSM_EXPAND * D_MODEL
SSM_HEAD_DIM = 64
SSM_HEADS = D_INNER // SSM_HEAD_DIM
SSM_GROUPS = 8
SSM_STATE = 128
SSM_CONV = 4
SSM_CHUNK = 128
XBC_DIM = D_INNER + 2 * SSM_GROUPS * SSM_STATE
SC_DIM = D_MODEL
SC_CONV = 3
D_FF = 5632
FFN_CONV = 3
PLE_DIM = 256
EPS = 1e-6
IN_SPLITS = (D_INNER, XBC_DIM, SSM_HEADS, SC_DIM, SC_DIM, SC_DIM, D_MODEL, D_MODEL)
IN_DIM = sum(IN_SPLITS)

kernel_name = "hybrid_ssd_shortconv_convffn_step"

def split_last(t, sizes):
    idx = np.cumsum(sizes)[:-1].tolist()
    return jnp.split(t, idx, axis=-1)

def rmsnorm(x, g):
    xf = x.astype(jnp.float32)
    y = xf * lax.rsqrt(jnp.mean(xf * xf, axis=-1, keepdims=True) + EPS)
    return (y * g.astype(jnp.float32)).astype(x.dtype)

def causal_dwconv(x, past, w, b=None):
    K = w.shape[0]
    L = x.shape[1]
    xp = jnp.concatenate([past.astype(x.dtype), x], axis=1)
    y = xp[:, 0:L] * w[0]
    for k in range(1, K):
        y = y + xp[:, k:k + L] * w[k]
    if b is not None:
        y = y + b
    return y, xp[:, L:]

def ssd_scan(x, dt, A, Bm, Cm, h0):
    b, L = x.shape[0], x.shape[1]
    G, R, P, N = SSM_GROUPS, SSM_HEADS // SSM_GROUPS, SSM_HEAD_DIM, SSM_STATE
    Q = min(SSM_CHUNK, L)
    nc = -(-L // Q)
    pad = nc * Q - L
    if pad:
        padt = lambda t: jnp.pad(t, [(0, 0), (0, pad)] + [(0, 0)] * (t.ndim - 2))
        x, dt, Bm, Cm = padt(x), padt(dt), padt(Bm), padt(Cm)
    x = x.reshape(b, nc, Q, G, R, P)
    dt = dt.reshape(b, nc, Q, G, R)
    Bm = Bm.reshape(b, nc, Q, G, N)
    Cm = Cm.reshape(b, nc, Q, G, N)
    Acum = jnp.cumsum(dt * A.reshape(G, R), axis=2)
    seg = Acum[:, :, :, None] - Acum[:, :, None]
    causal = jnp.tril(jnp.ones((Q, Q), dtype=bool))[:, :, None, None]
    Lmat = jnp.exp(jnp.where(causal, seg, -jnp.inf))
    CB = jnp.einsum('bclgn,bcsgn->bclsg', Cm, Bm)
    Wm = CB[..., None] * Lmat * dt[:, :, None]
    y_diag = jnp.einsum('bclsgr,bcsgrp->bclgrp', Wm, x)
    decay_end = jnp.exp(Acum[:, :, -1:] - Acum)
    chunk_states = jnp.einsum('bclgn,bclgr,bclgrp->bcgrpn', Bm, decay_end * dt, x)
    chunk_decay = jnp.exp(Acum[:, :, -1])

    def step(h, inp):
        s, d = inp
        return d[..., None, None] * h + s, h

    hT, h_prev = lax.scan(step, h0.reshape(b, G, R, P, N),
                          (jnp.moveaxis(chunk_states, 1, 0), jnp.moveaxis(chunk_decay, 1, 0)))
    h_prev = jnp.moveaxis(h_prev, 0, 1)
    y_off = jnp.einsum('bclgn,bcgrpn,bclgr->bclgrp', Cm, h_prev, jnp.exp(Acum))
    y = (y_diag + y_off).reshape(b, nc * Q, SSM_HEADS, P)[:, :L]
    return y, hT.reshape(b, SSM_HEADS, P, N)

def trunk_layer(x, pe, ssm0, xbc0, sc0, ffn0,
                norm_mix, w_in, ssm_conv_w, ssm_conv_b, ssm_dt_bias, ssm_a_log, ssm_d, ssm_norm,
                w_ssm_out, sc_conv_w, w_sc_out, w_o, norm_ffn, w_ffn_gate, w_ffn_up,
                ffn_conv_w, ffn_conv_b, w_ffn_down, norm_ple, w_ple, w_ple_gate):
    f32 = jnp.float32
    b, L, _ = x.shape
    n1 = rmsnorm(x, norm_mix)
    proj = n1 @ w_in
    z, xbc, dt_raw, sc_b, sc_c, sc_h, gate_a, gate_b = split_last(proj, IN_SPLITS)

    xbc_c, xbc_state = causal_dwconv(xbc, xbc0, ssm_conv_w, ssm_conv_b)
    xbc_c = jax.nn.silu(xbc_c)
    xs, Bm, Cm = split_last(xbc_c, (D_INNER, SSM_GROUPS * SSM_STATE, SSM_GROUPS * SSM_STATE))
    xs_h = xs.reshape(b, L, SSM_HEADS, SSM_HEAD_DIM).astype(f32)
    dt = jax.nn.softplus(dt_raw.astype(f32) + ssm_dt_bias.astype(f32))
    A = -jnp.exp(ssm_a_log.astype(f32))
    y, h_new = ssd_scan(xs_h, dt, A,
                        Bm.reshape(b, L, SSM_GROUPS, SSM_STATE).astype(f32),
                        Cm.reshape(b, L, SSM_GROUPS, SSM_STATE).astype(f32),
                        ssm0.astype(f32))
    y = y + ssm_d.astype(f32)[:, None] * xs_h
    y = y.reshape(b, L, D_INNER) * jax.nn.silu(z.astype(f32))
    yg = y.reshape(b, L, SSM_GROUPS, D_INNER // SSM_GROUPS)
    yg = yg * lax.rsqrt(jnp.mean(yg * yg, axis=-1, keepdims=True) + EPS)
    y = (yg.reshape(b, L, D_INNER) * ssm_norm.astype(f32)).astype(x.dtype)
    branch_a = y @ w_ssm_out

    sc_conv, sc_state = causal_dwconv(sc_c * sc_h, sc0, sc_conv_w)
    branch_b = (sc_b * sc_conv) @ w_sc_out

    mixed = jax.nn.sigmoid(gate_a) * branch_a + jax.nn.sigmoid(gate_b) * branch_b
    x = x + mixed @ w_o

    n2 = rmsnorm(x, norm_ffn)
    g_up = n2 @ w_ffn_gate
    g_conv, ffn_state = causal_dwconv(g_up, ffn0, ffn_conv_w, ffn_conv_b)
    x = x + (jax.nn.silu(g_conv) * (n2 @ w_ffn_up)) @ w_ffn_down

    n3 = rmsnorm(x, norm_ple)
    x = x + (pe.astype(x.dtype) @ w_ple) * jax.nn.sigmoid(n3 @ w_ple_gate)
    return x, h_new.astype(ssm0.dtype), xbc_state, sc_state, ffn_state

def setup_inputs(seed: int = 0) -> dict:
    key = jax.random.key(seed)
    ks = iter(jax.random.split(key, 48))
    f32 = jnp.float32

    def nrm(shape, scale=1.0):
        return jax.random.normal(next(ks), shape, f32) * scale

    def gain(shape):
        return 1.0 + nrm(shape, 0.05)

    log_dt = jax.random.uniform(next(ks), (DEPTH, SSM_HEADS), f32,
                                minval=math.log(1e-3), maxval=math.log(1e-1))
    dt0 = jnp.exp(log_dt)
    dt_bias = dt0 + jnp.log(-jnp.expm1(-dt0))
    a_log = jnp.log(jax.random.uniform(next(ks), (DEPTH, SSM_HEADS), f32, minval=1.0, maxval=16.0))
    return {
        'x_prompt': nrm((BATCH, SEQ, D_MODEL)),
        'x_sample': nrm((DEC_BATCH, DEC_SEQ, D_MODEL)),
        'state_ssm': nrm((DEPTH, DEC_BATCH, SSM_HEADS, SSM_HEAD_DIM, SSM_STATE), 0.1),
        'state_ssm_conv': nrm((DEPTH, DEC_BATCH, SSM_CONV - 1, XBC_DIM)),
        'state_short_conv': nrm((DEPTH, DEC_BATCH, SC_CONV - 1, SC_DIM)),
        'state_ffn_conv': nrm((DEPTH, DEC_BATCH, FFN_CONV - 1, D_FF)),
        'p_prompt': nrm((DEPTH, BATCH, SEQ, PLE_DIM)),
        'p_sample': nrm((DEPTH, DEC_BATCH, DEC_SEQ, PLE_DIM)),
        'norm_mix': gain((DEPTH, D_MODEL)),
        'w_in': nrm((DEPTH, D_MODEL, IN_DIM), D_MODEL ** -0.5),
        'ssm_conv_w': nrm((DEPTH, SSM_CONV, XBC_DIM), 0.5),
        'ssm_conv_b': nrm((DEPTH, XBC_DIM), 0.02),
        'ssm_dt_bias': dt_bias,
        'ssm_a_log': a_log,
        'ssm_d': gain((DEPTH, SSM_HEADS)),
        'ssm_norm': gain((DEPTH, D_INNER)),
        'w_ssm_out': nrm((DEPTH, D_INNER, D_MODEL), D_INNER ** -0.5),
        'sc_conv_w': nrm((DEPTH, SC_CONV, SC_DIM), SC_CONV ** -0.5),
        'w_sc_out': nrm((DEPTH, SC_DIM, D_MODEL), SC_DIM ** -0.5),
        'w_o': nrm((DEPTH, D_MODEL, D_MODEL), D_MODEL ** -0.5),
        'norm_ffn': gain((DEPTH, D_MODEL)),
        'w_ffn_gate': nrm((DEPTH, D_MODEL, D_FF), D_MODEL ** -0.5),
        'w_ffn_up': nrm((DEPTH, D_MODEL, D_FF), D_MODEL ** -0.5),
        'ffn_conv_w': nrm((DEPTH, FFN_CONV, D_FF), FFN_CONV ** -0.5),
        'ffn_conv_b': nrm((DEPTH, D_FF), 0.02),
        'w_ffn_down': nrm((DEPTH, D_FF, D_MODEL), D_FF ** -0.5),
        'norm_ple': gain((DEPTH, D_MODEL)),
        'w_ple': nrm((DEPTH, PLE_DIM, D_MODEL), PLE_DIM ** -0.5),
        'w_ple_gate': nrm((DEPTH, D_MODEL, D_MODEL), D_MODEL ** -0.5),
        'norm_final': gain((D_MODEL,)),
    }

def reference(x_prompt, x_sample, state_ssm, state_ssm_conv, state_short_conv, state_ffn_conv,
              p_prompt, p_sample, norm_mix, w_in, ssm_conv_w, ssm_conv_b, ssm_dt_bias, ssm_a_log,
              ssm_d, ssm_norm, w_ssm_out, sc_conv_w, w_sc_out, w_o, norm_ffn, w_ffn_gate, w_ffn_up,
              ffn_conv_w, ffn_conv_b, w_ffn_down, norm_ple, w_ple, w_ple_gate, norm_final):
    dt_p = x_prompt.dtype
    yp, ys = x_prompt, x_sample
    ssm_p, ssm_s, xbc_p, xbc_s, sc_p, sc_s, ffn_p, ffn_s = [], [], [], [], [], [], [], []
    for i in range(DEPTH):
        lw = (norm_mix[i], w_in[i], ssm_conv_w[i], ssm_conv_b[i], ssm_dt_bias[i], ssm_a_log[i],
              ssm_d[i], ssm_norm[i], w_ssm_out[i], sc_conv_w[i], w_sc_out[i], w_o[i], norm_ffn[i],
              w_ffn_gate[i], w_ffn_up[i], ffn_conv_w[i], ffn_conv_b[i], w_ffn_down[i], norm_ple[i],
              w_ple[i], w_ple_gate[i])
        yp, s0, s1, s2, s3 = trunk_layer(
            yp, p_prompt[i],
            jnp.zeros((BATCH, SSM_HEADS, SSM_HEAD_DIM, SSM_STATE), dt_p),
            jnp.zeros((BATCH, SSM_CONV - 1, XBC_DIM), dt_p),
            jnp.zeros((BATCH, SC_CONV - 1, SC_DIM), dt_p),
            jnp.zeros((BATCH, FFN_CONV - 1, D_FF), dt_p),
            *lw)
        ssm_p.append(s0); xbc_p.append(s1); sc_p.append(s2); ffn_p.append(s3)
        ys, t0, t1, t2, t3 = trunk_layer(
            ys, p_sample[i], state_ssm[i], state_ssm_conv[i], state_short_conv[i], state_ffn_conv[i],
            *lw)
        ssm_s.append(t0); xbc_s.append(t1); sc_s.append(t2); ffn_s.append(t3)
    y_prompt = rmsnorm(yp, norm_final)
    y_sample = rmsnorm(ys, norm_final)
    return (y_prompt, y_sample,
            jnp.stack(ssm_p), jnp.stack(ssm_s),
            jnp.stack(xbc_p), jnp.stack(xbc_s),
            jnp.stack(sc_p), jnp.stack(sc_s),
            jnp.stack(ffn_p), jnp.stack(ffn_s))


_drawn_inputs = setup_inputs


def setup_inputs(seed=0):
    import zlib

    import numpy as np

    out = dict(_drawn_inputs(seed))
    spreads = {}
    factors = {'ssm_d': 4.308, 'ffn_conv_b': 6.966, 'norm_ple': 8.0}
    for name, (base, spread) in spreads.items():
        noise = np.random.default_rng([zlib.crc32(name.encode()), seed]).standard_normal(out[name].shape)
        drawn = base * np.exp(spread * noise) if base else spread * noise
        out[name] = __import__('jax').numpy.asarray(drawn.astype(out[name].dtype))
    for name, factor in factors.items():
        out[name] = (out[name] * factor).astype(out[name].dtype)
    return out
```

```python
import concourse.bass as bass
from concourse import mybir
from contextlib import ExitStack

F32 = mybir.dt.float32
F32R = mybir.dt.float32r
ALU = mybir.AluOpType
ACT = mybir.ActivationFunctionType

P = 128
DM = 2048
SEQ = 256
NB, LB = 8, 8
NS = NB * LB
NT = SEQ + NS
DI = 4096
HEADS, HD, GROUPS, NST = 64, 64, 8, 128
HPG = HEADS // GROUPS
XBC = DI + 2 * GROUPS * NST
DFF = 5632
PLE = 256
EPS = 1e-6
KM = DM // P
K_X, K_SC, K_F = 4, 3, 3

COL_Z = 0
COL_XBC = DI
COL_DT = COL_XBC + XBC
COL_SCB = COL_DT + HEADS
COL_SCC = COL_SCB + DM
COL_SCH = COL_SCC + DM
COL_GA = COL_SCH + DM
COL_GB = COL_GA + DM

PW = 1024
RING = 4
AHEAD = 3

def padded(taps):
    first = SEQ + taps - 1
    step = LB + taps - 1
    return first, step, first + NB * step


PARAMS = {}
_n = 0
for _name, _rows in (("cx", K_X * XBC // P), ("cxb", XBC // P), ("gy", DI // P), ("g1", KM),
                     ("cs", K_SC * KM), ("g2", KM), ("cf", K_F * DFF // P), ("cfb", DFF // P),
                     ("g3", KM), ("g4", KM)):
    PARAMS[_name] = (_n, _rows)
    _n += _rows
N_PARAMS = _n
PARAM_BLOCKS = -(-N_PARAMS // P)

PARAM_SOURCE = {"cx": "ssm_conv_w", "cxb": "ssm_conv_b", "gy": "ssm_norm", "g1": "norm_mix",
                "cs": "sc_conv_w", "g2": "norm_ffn", "cf": "ffn_conv_w", "cfb": "ffn_conv_b",
                "g3": "norm_ple", "g4": "norm_final"}

OUT8 = [("out", k) for k in range(8)]


class Seg:

    def __init__(self, name, chunk0, start, stop, steps, outs=None):
        self.name, self.chunk0, self.start, self.stop, self.steps = name, chunk0, start, stop, steps
        self.outs = outs
        self.loop = stop - start > 1
        self.per = sum(pieces_of(s) for s in steps)
        assert not self.loop or self.per % RING == 0


def pieces_of(step):
    return {"out": 1, "ple": 1, "unit": 2}.get(step[0], 0)


def ssm_steps(first):
    head = [("unit", "x", 0)] + ([] if first else [("norm", 0)]) + [("unit", "x", 1)]
    if first:
        head += [("dtab", 0), ("unit", "x", 2)]
    else:
        head += [("unit", "x", 2)] + OUT8
    tail = [("unit", "x", 3), ("unit", "x", 4), ("unit", "x", 5)]
    return head + tail + [("unit", "z", 0), ("ssd1", 0), ("unit", "z", 1), ("ssd2", 0), ("ssd3", 0),
                          ("pair", 0), ("unit", "z", 2), ("pair", 1), ("unit", "z", 3), ("pair", 2), ("pair", 3)]


def sc_steps(first):
    steps = [("unit", "c", 0)] + ([("norm", 0)] if first else []) + [("unit", "h", 0), ("unit", "b", 0)]
    steps += OUT8 + [("fin", 0)]
    for j in (1, 2, 3):
        steps += [("unit", "c", j), ("unit", "h", j), ("unit", "b", j), ("fin", j)]
    return steps


def mix_steps():
    steps = [("unit", "ga", 0), ("unit", "gb", 0)] + OUT8 + [("mix", 0), ("fin", 0)]
    for j in (1, 2, 3):
        steps += [("unit", "ga", j), ("unit", "gb", j), ("mix", j), ("fin", j)]
    return steps


def ffn_steps(first):
    steps = [("unit", "g", 0), ("unit", "u", 0)] + ([] if first else OUT8) + [("fin", 0)]
    for j in (1, 2, 3):
        steps += [("unit", "g", j), ("unit", "u", j), ("fin", j)]
    return steps


N_F = DFF // P // 4
C_SC, C_MIX, C_F = GROUPS, GROUPS + 4, GROUPS + 8
PLE_STEPS = [("unit", "pg", j) for j in range(4)]
SEGS = [
    Seg("prologue", 0, 0, 1, [("start", 0), ("unit", "dt", 0)]),
    Seg("ssm", 0, 0, 1, ssm_steps(True)),
    Seg("ssm", 0, 1, GROUPS, ssm_steps(False), "ssm"),
    Seg("sc", C_SC, 0, 1, sc_steps(True), "ssm"),
    Seg("sc", C_SC, 1, 4, sc_steps(False), "sc"),
    Seg("mix", C_MIX, 0, 1, mix_steps(), "sc"),
    Seg("mix", C_MIX, 1, 4, mix_steps(), "mix"),
    Seg("mixend", C_MIX, 4, 5, OUT8 + [("ple", 0), ("rsum", 2), ("ple", 1), ("rms", 2)], "mix"),
    Seg("ffn", C_F, 0, 1, ffn_steps(True)),
    Seg("ffn", C_F, 1, N_F, ffn_steps(False), "ffn"),
    Seg("ffnend", C_F, N_F, N_F + 1, OUT8 + [("ple", 2), ("rsum", 3), ("ple", 3), ("rms", 3)], "ffn"),
    Seg("ple", 0, 0, 3, PLE_STEPS),
    Seg("ple", 0, 3, 4, PLE_STEPS),
    Seg("finish", 0, 0, 1, [("rsum", 4), ("rms", 4), ("end", 0)]),
]
_p = 0
for _s in SEGS:
    _s.piece0 = _p
    _p += _s.per * (_s.stop - _s.start)
TOTAL_PIECES = _p


def hybrid_decoder(nc, ins, outs, scratch):
    ctx = ExitStack()
    with ctx:
        def sem(name):
            return ctx.enter_context(nc.semaphore(name))

        def fixed(name, shape, dt=F32):
            return ctx.enter_context(nc.sbuf_tensor(name, shape, dt))

        def region():
            return ExitStack()

        raw = [fixed(f"raw{s}", [P, PW]) for s in range(RING)]
        whi = [fixed(f"whi{s}", [P, PW], F32R) for s in range(RING)]
        wlo = [fixed(f"wlo{s}", [P, PW], F32R) for s in range(RING)]
        n_hi = fixed("n_hi", [P, KM, NT], F32R)
        n_lo = fixed("n_lo", [P, KM, NT], F32R)
        c_hi = fixed("c_hi", [P, 4, NT], F32R)
        c_lo = fixed("c_lo", [P, 4, NT], F32R)
        chunk = fixed("chunk", [P, 4, NT])
        acc_a = fixed("acc_a", [P, KM, NT])
        ident = fixed("ident", [P, P])
        ones = fixed("ones", [P, P])
        tri = fixed("tri", [P, P])
        after = fixed("after", [P, P])
        tri_s = fixed("tri_s", [NS, NS + NB])
        after_s = fixed("after_s", [NS, NS])
        ptab = fixed("ptab", [P, N_PARAMS])
        sstate = fixed("sstate", [P, NB * (K_SC - 1), KM])
        stail = fixed("stail", [P, NB + 1, K_SC - 1, KM])
        xtail = fixed("xtail", [P, NB + 1, K_X - 1, XBC // P])
        var = fixed("var", [P, NT])
        rstd = fixed("rstd", [P, NT])

        FX, SX, WX = padded(K_X)
        FS, SS, WS = padded(K_SC)
        N_CX = WX - K_X + 1
        N_CS = WS - K_SC + 1

        ssm = region()

        def s1(name, shape, dt=F32):
            return ssm.enter_context(nc.sbuf_tensor(name, shape, dt))

        N_KC = 13
        heads_tab = s1("heads_tab", [P, GROUPS, N_KC, HPG])
        hvec = s1("hvec", [HEADS, 3])
        dcol = s1("dcol", [P, HEADS // 2])
        xstate = s1("xstate", [P, NB * (K_X - 1), XBC // P])

        pro = region()

        def s0(name, shape, dt=F32):
            return pro.enter_context(nc.sbuf_tensor(name, shape, dt))

        xrow = s0("xrow", [P, 3, DM])
        xt0 = s0("xt0", [P, KM, NT])
        prow = s0("prow", [P, PARAM_BLOCKS, P])
        xsrow = s0("xsrow", [P, 9, P])
        ssrow = s0("ssrow", [P, 2, P])
        sq0 = s0("sq0", [P, 2, 4, NT])
        nt0 = s0("nt0", [P, 2, 4, NT])
        pro.close()

        xs = s1("xs", [P, 4, NT])
        bc = s1("bc", [P, 2, NT])
        zs = s1("zs", [P, 4, NT])
        xpad_mem = s1("xpad", [P, 2 * WX + 10])
        xpad = [xpad_mem[:, i * WX:i * WX + WX + 9] for i in range(2)]
        cv = s1("cv", [P, 2, WX])
        xdt = s1("xdt", [P, 3, 4 * P])
        xwe = s1("xwe", [P, 3, 4 * P])
        xwf = s1("xwf", [P, 4 * P])
        bt = s1("bt", [P, 3, P])
        bblk = s1("bblk", [NS, NB, P])
        cbm = s1("cbm", [P, 3, P])
        wm = s1("wm", [P, 5, 512])
        ea = s1("ea", [P, 4, P + NS + NB])
        h1t = s1("h1t", [P, 512])
        hfin = s1("hfin", [P, 4, P])
        h0 = [s1(f"h0_{i}", [P, NB, P]) for i in range(2)]
        hn = [s1(f"hn_{i}", [P, NB, P]) for i in range(2)]
        h0t = s1("h0t", [P, NB, P])
        yoffs = s1("yoffs", [P, P + NS])
        hcol = s1("hcol", [P, N_KC, HPG])
        gcol = s1("gcol", [P, K_X + 1, 6])
        gnrm = s1("gnrm", [P, 4])
        gd = s1("gd", [P, 4])
        ssm.close()

        post = region()

        def s2(name, shape, dt=F32):
            return post.enter_context(nc.sbuf_tensor(name, shape, dt))

        acc_b = s2("acc_b", [P, KM, NT])
        xt = s2("xt", [P, KM, NT])
        cmul = s2("cmul", [P, 2, NT])
        spad_mem = s2("spad", [P, 2 * WS + 10])
        spad = [spad_mem[:, i * WS:i * WS + WS + 9] for i in range(2)]
        scv = s2("scv", [P, 2, WS])
        scol = s2("scol", [P, K_F + 1, 4])
        sig_a = s2("sig_a", [P, 2, NT])
        sig_b = s2("sig_b", [P, 2, NT])
        fstate = s2("fstate", [P, NB * (K_F - 1), DFF // P])
        ftail = s2("ftail", [P, NB + 1, K_F - 1, DFF // P])
        sq = s2("sq", [P, 2, 4, NT])
        nt = s2("nt", [P, 2, 4, NT])
        peT_hi = s2("peT_hi", [P, 2, NT], F32R)
        peT_lo = s2("peT_lo", [P, 2, NT], F32R)
        free_b = acc_b[:].rearrange("p a b -> p (a b)")
        fsrow = free_b[:, 32 * P:38 * P].rearrange("p (r f) -> p r f", f=P)
        trow = free_b[:, 0:21 * P].rearrange("p (r f) -> p r f", f=P)
        perow = free_b[:, 21 * P:21 * P + 3 * PLE].rearrange("p (c f) -> p c f", f=PLE)
        pef = free_b[:, 21 * P + 3 * PLE:21 * P + 3 * PLE + 2 * NT].rearrange("p (c f) -> p c f", f=NT)
        yrow = [sq[:].rearrange("p a b c -> p (a b c)")[:, 0:DM], nt[:].rearrange("p a b c -> p (a b c)")[:, 0:DM],
                free_b[:, 0:DM]]
        post.close()

        ps = ctx.enter_context(nc.psum_tensor("ps", [P, 8, 512], F32))
        RMS_BANK, VS_BANK, DT_BANK = (None, 3, 7, 7, 4), 2, 7
        sq_pair, sq_sum = [sq[:, i, 0:2, :] for i in range(2)], sq[:, 0, 2:4, :]
        SQUARES = (None, 0, 4, 12, 20)
        ADDED = (None, 0, 0, 7, 14)
        OUTS_BEFORE = (None, 0, 8 * C_F, 8 * (C_F + N_F))
        SUMS = (None, 4, 5, 6, 7)
        QUADS = ((0, 7), (0, 2), (1, 3), (1, 4), (2, 5))
        HN_BANKS = (7, 2)
        CONSTS, DVE_LINKS = 12, {"ssm": 30, "sc": 8, "mix": 4, "ffn": 8, "ple": 4}
        N_CONSTS = CONSTS
        flat3 = "p a b -> p (a b)"
        xst, sst = xstate[:].rearrange(flat3), sstate[:].rearrange(flat3)
        TAB_COPIES = [(ptab[:, 0:512], 512), (ptab[:, 512:N_PARAMS], N_PARAMS - 512),
                      (xst[:, 0:512], 512), (xst[:, 512:1024], 512), (xst[:, 1024:1152], 128),
                      (sst[:, 0:256], 256)]
        TAB_BANKS = (0, 1, 2, 4, 5, 6)
        TAB_SOURCES = [[(prow[:, b, :], P) for b in range(4)], [(prow[0:N_PARAMS - 512, 4, :], N_PARAMS - 512)],
                       [(xsrow[:, b, :], P) for b in range(4)], [(xsrow[:, b, :], P) for b in range(4, 8)],
                       [(xsrow[:, 8, :], P)], [(ssrow[:, b, :], P) for b in range(2)]]
        N_PARAM_LOADS = 2 + sum(1 for row, rows in PARAMS.values() for b in range(PARAM_BLOCKS)
                                if max(row, b * P) < min(row + rows, b * P + P))
        OUT_BANKS = (4, 6)

        ends = [seg for seg in SEGS if seg.name in ("mixend", "ffnend")]
        PLE_PIECES = [seg.piece0 + 8 + i for seg in ends for i in range(2)]

        raw_loaded = [sem(f"raw_loaded{s}") for s in range(RING)]
        hi_split = sem("hi_split")
        lo_split = sem("lo_split")
        multiplied = sem("multiplied")
        out_added = sem("out_added")
        f_ready = sem("f_ready")
        c_hi_ready = sem("c_hi_ready")
        c_ready = sem("c_ready")
        loads_let_go = sem("loads_let_go")
        x_loaded, params_loaded, cols_loaded = sem("x_loaded"), sem("params_loaded"), sem("cols_loaded")
        consts_ready = sem("consts_ready")
        x_turned, x_kept_a, x_kept_v = sem("x_turned"), sem("x_kept_a"), sem("x_kept_v")
        tab_turned, tab_kept = sem("tab_turned"), sem("tab_kept")
        x_saved, x_back = sem("x_saved"), sem("x_back")
        sq_ready, sq_added = sem("sq_ready"), sem("sq_added")
        sq_summed, var_ready, ysum_ready = sem("sq_summed"), sem("var_ready"), sem("ysum_ready")
        rstd_ready, n_full, n_hi_ready, n_ready = sem("rstd_ready"), sem("n_full"), sem("n_hi_ready"), sem("n_ready")
        dt_min, dt_exp, a_exp, dt_done = sem("dt_min"), sem("dt_exp"), sem("a_exp"), sem("dt_done")
        dt_turned, a_kept, dt_sums, dt_decay, heads_ready = (
            sem("dt_turned"), sem("a_kept"), sem("dt_sums"), sem("dt_decay"), sem("heads_ready"))
        gcol_ready, hcol_ready, gnrm_ready = sem("gcol_ready"), sem("hcol_ready"), sem("gnrm_ready")
        xpad_filled, xpast, xtail_kept = sem("xpad_filled"), sem("xpast"), sem("xtail_kept")
        conv_done, xs_ready, z_ready = sem("conv_done"), sem("xs_ready"), sem("z_ready")
        xt_done, bt_done, cb_done, q_done = sem("xt_done"), sem("bt_done"), sem("cb_done"), sem("q_done")
        xw_ready, bt_kept, cbm_ready, bblk_ready = sem("xw_ready"), sem("bt_kept"), sem("cbm_ready"), sem("bblk_ready")
        q_min, q_exp, w_ready = sem("q_min"), sem("q_exp"), sem("w_ready")
        ea_done, ea_exp = sem("ea_done"), sem("ea_exp")
        h1_done, h1_kept, hfin_stored = sem("h1_done"), sem("h1_kept"), sem("hfin_stored")
        h0_loaded = [sem(f"h0_loaded{i}") for i in range(2)]
        hn_stored = [sem(f"hn_stored{i}") for i in range(2)]
        t_done, t_kept = sem("t_done"), sem("t_kept")
        yd_done, hn_done, yoff_done = sem("yd_done"), sem("hn_done"), sem("yoff_done")
        yg_ready, hd_done, hn_added = sem("yg_ready"), sem("hd_done"), sem("hn_added")
        ysq_ready, vs_done, vsum_read, vinv, yrstd = (
            sem("ysq_ready"), sem("vs_done"), sem("vsum_read"), sem("vinv"), sem("yrstd"))
        cmul_ready, prod_done, spast, stail_kept, sconv_done = (
            sem("cmul_ready"), sem("prod_done"), sem("spast"), sem("stail_kept"), sem("sconv_done"))
        spad_filled, gact_ready = sem("spad_filled"), sem("gact_ready")
        sigs = sem("sigs")
        post_zero, ftab_loaded, ftab_turned, ftab_kept = (
            sem("post_zero"), sem("ftab_loaded"), sem("ftab_turned"), sem("ftab_kept"))
        pe_loaded, pe_turned, pe_kept, pe_hi, pe_ready, ple_kept, ple_added = (
            sem("pe_loaded"), sem("pe_turned"), sem("pe_kept"), sem("pe_hi"), sem("pe_ready"),
            sem("ple_kept"), sem("ple_added"))
        tail_turned, tail_kept, tails_stored = sem("tail_turned"), sem("tail_kept"), sem("tails_stored")
        y_full, y_turned, y_kept_a, y_kept_v, y_stored = (
            sem("y_full"), sem("y_turned"), sem("y_kept_a"), sem("y_kept_v"), sem("y_stored"))
        act_own, dve_own, pool_own = sem("act_own"), sem("dve_own"), sem("pool_own")

        block = ctx.enter_context(nc.Block())

        def wait(eng, s, value):
            if not isinstance(value, int) or value > 0:
                eng.wait_ge(s, value)

        def first_piece(seg, it):
            return seg.piece0 + (it - seg.start) * seg.per

        def at(i, n=1, size=1):
            return slice(i * size, (i + n) * size) if isinstance(i, int) else bass.ds(i * size, n * size)

        class Own:

            def __init__(self, eng, s):
                self.eng, self.s, self.n, self.round = eng, s, 0, 0

            def __call__(self, ins):
                self.n += 1
                ins.then_inc(self.s, 1)
                self.eng.wait_ge(self.s, self.n + self.round)

            def enter(self, it, start, per):
                self.round, self.n0, self.per = (it - start) * per, self.n, per

            def leave(self, rounds):
                assert self.n - self.n0 == self.per, f"links per round: {self.n - self.n0}"
                self.n += (rounds - 1) * self.per
                self.round = 0

        def walk(eng, visit, own=None, links=None):
            for seg in SEGS:
                if seg.loop:
                    with eng.Fori(seg.start, seg.stop) as it:
                        if own:
                            own.enter(it, seg.start, links.get(seg.name, 0))
                        visit(seg, it)
                        if own:
                            own.leave(seg.stop - seg.start)
                else:
                    visit(seg, seg.start)

        def tiles(view, i):
            return view[:, i * P:(i + 1) * P]

        def pw(seg, it, pos):
            return first_piece(seg, it) + pos + 1

        def prompt_of(pad, taps, shift=0):
            return pad[:, shift:shift + SEQ]

        def samples_of(pad, taps, shift=0, n=LB):
            first, step, _ = padded(taps)
            return pad[:, first:first + NB * step].rearrange("p (b l) -> p b l", l=step)[:, :, shift:shift + n]

        def last_rows(pad, taps):
            step = padded(taps)[1]
            return pad[:, SEQ:SEQ + (NB + 1) * step].rearrange("p (b l) -> p b l", l=step)[:, :, 0:taps - 1]

        def kt(w):
            return w.rearrange("(k p) n -> p k n", p=P)

        w_in, w_ssm, w_sc = kt(ins["w_in"][0]), kt(ins["w_ssm_out"][0]), kt(ins["w_sc_out"][0])
        w_o, w_fg, w_fu = kt(ins["w_o"][0]), kt(ins["w_ffn_gate"][0]), kt(ins["w_ffn_up"][0])
        w_fd, w_p, w_pg = kt(ins["w_ffn_down"][0]), kt(ins["w_ple"][0]), kt(ins["w_ple_gate"][0])
        out_w = {"ssm": (w_ssm, 0), "sc": (w_sc, C_SC), "mix": (w_o, C_MIX), "ffn": (w_fd, C_F)}

        def unit_columns(step, it):
            kind, j = step[1], (step[2] if len(step) > 2 else 0)
            if kind == "x" and j < 4:
                return w_in, COL_XBC + (4 * it + j) * P
            if kind == "x":
                return w_in, COL_XBC + DI + (j - 4) * GROUPS * NST + it * P
            if kind == "dt":
                return w_in, COL_DT
            col = {"z": COL_Z, "c": COL_SCC, "h": COL_SCH, "b": COL_SCB, "ga": COL_GA, "gb": COL_GB}
            if kind in col:
                return w_in, col[kind] + (4 * it + j) * P
            return {"g": w_fg, "u": w_fu, "pg": w_pg}[kind], (4 * it + j) * P

        def pieces(seg, it):
            pos = 0
            for step in seg.steps:
                if step[0] == "unit":
                    w, col = unit_columns(step, it)
                    for half in range(2):
                        yield pos, w[:, 8 * half:8 * half + 8, at(col, P)], P
                        pos += 1
                elif step[0] == "out":
                    w, c0 = out_w[seg.outs]
                    kt0 = 4 * (seg.chunk0 + it - 1 - c0)
                    yield pos, w[:, at(kt0, 4), 256 * step[1]:256 * step[1] + 256], 256
                    pos += 1
                elif step[0] == "ple":
                    yield pos, w_p[:, :, 512 * step[1]:512 * step[1] + 512], 512
                    pos += 1

        ffn_past = ins["state_ffn_conv"][0].rearrange("b k (t f) -> (b k t) f", f=P)
        TAILS = [(xtail, 0, (NB + 1) * (K_X - 1) * (XBC // P), "xbc"),
                 (stail, 11, (NB + 1) * (K_SC - 1) * KM, "sc"),
                 (ftail, 14, (NB + 1) * (K_F - 1) * (DFF // P), "ffn")]

        def tail_blocks():
            for table, first, rows, _ in TAILS:
                flat = table[:].rearrange("p i k t -> p (i k t)")
                for r in range(0, rows, P):
                    n = min(P, rows - r)
                    yield first + r // P, flat[:, r:r + n], n

        TAIL_BLOCKS = list(tail_blocks())
        N_TAIL_BLOCKS = len(TAIL_BLOCKS)
        TAIL_FOURS = [(b % 4, [(m, n) for m, _, n in TAIL_BLOCKS if m // 4 == b])
                      for b in range(-(-N_TAIL_BLOCKS // 4))]

        def tail_stores():
            for _, first, rows, name in TAILS:
                n_prompt = rows // (NB + 1)
                for out_name, lo, hi in ((name + "_prompt", 0, n_prompt), (name + "_sample", n_prompt, rows)):
                    dst = outs[out_name][0].rearrange("b k (t f) -> (b k t) f", f=P)
                    r = lo
                    while r < hi:
                        if r % P == 0 and hi - r >= P:
                            n = (hi - r) // P
                            yield (dst[r - lo:r - lo + n * P].rearrange("(m p) f -> p m f", p=P),
                                   trow[:, first + r // P:first + r // P + n, :])
                            r += n * P
                        else:
                            n = min(P - r % P, hi - r)
                            yield dst[r - lo:r - lo + n], trow[r % P:r % P + n, first + r // P, :]
                            r += n

        def ssm_over(eng):
            eng.wait_ge(yg_ready, 4 * GROUPS)
            eng.wait_ge(ysq_ready, 4 * GROUPS)
            eng.wait_ge(hn_added, 8 * GROUPS)
            eng.wait_ge(hd_done, 8 * GROUPS)
            eng.wait_ge(xtail_kept, 6 * GROUPS)
            eng.wait_ge(hfin_stored, 16 * GROUPS)
            for i in range(2):
                eng.wait_ge(hn_stored[i], 16 * 2 * GROUPS)

        @block.sync
        def _(sp):
            x_rows = ins["x_prompt"][0].rearrange("(c p) d -> p c d", p=P)
            sp.dma_start(xrow[:, 0:2, :], x_rows).then_inc(x_loaded, 16)
            sp.dma_start(xrow[0:NS, 2, :], ins["x_sample"].rearrange("b l d -> (b l) d")).then_inc(x_loaded, 16)

            def visit(seg, it):
                base = first_piece(seg, it)
                for pos, block_of_w, width in pieces(seg, it):
                    slot = (seg.piece0 + pos) % RING
                    if pos % 2 == 0:
                        wait(sp, lo_split, base + pos + 1 - RING + 1)
                        sp.sem_inc(loads_let_go, 1)
                    sp.dma_start(raw[slot][:].rearrange("p (k n) -> p k n", n=width),
                                 block_of_w).then_inc(raw_loaded[slot], 16)
            walk(sp, visit)
            sp.wait_ge(x_saved, 16)
            sp.wait_ge(hfin_stored, 16 * GROUPS)
            for i in range(2):
                sp.wait_ge(hn_stored[i], 16 * GROUPS * 2)
            sp.wait_ge(tails_stored, 16 * len(list(tail_stores())))
            sp.wait_ge(y_stored, 16 * 3)

        def raw_count(seg, it, pos):
            return 16 * ((seg.piece0 + pos) // RING + 1) + 16 * (seg.per // RING) * (it - seg.start)

        def split_steps(seg, it, step, pos):
            for n in range(pos, pos + pieces_of(step)):
                ahead = n + AHEAD
                if seg.loop or first_piece(seg, it) + ahead < TOTAL_PIECES:
                    yield (seg.piece0 + ahead) % RING, first_piece(seg, it) + ahead, ahead

        def run_steps(eng, seg, it, split, tasks):
            pos, outs_end = 0, None
            for step in seg.steps:
                split(seg, it, step, pos)
                if step[0] == "out":
                    outs_end = pos
                tasks(seg, it, step, pos, outs_end)
                pos += pieces_of(step)

        @block.scalar
        def _(act):
            own = Own(act, act_own)
            copy, activate = ACT.Copy, nc.scalar.activation
            for block_i in range(PARAM_BLOCKS):
                for name, (row, rows) in PARAMS.items():
                    lo, hi = max(row, block_i * P), min(row + rows, block_i * P + P)
                    if lo < hi:
                        src = ins[PARAM_SOURCE[name]]
                        src = src if len(src.shape) == 1 else src[0]
                        flat = src.rearrange("k n -> (k n)") if len(src.shape) == 2 else src
                        act.dma_start(prow[lo - block_i * P:hi - block_i * P, block_i, :],
                                      flat[(lo - row) * P:(hi - row) * P].rearrange("(r f) -> r f", f=P)
                                      ).then_inc(params_loaded, 16)
            act.dma_start(xsrow[:], ins["state_ssm_conv"][0].rearrange("b k (t f) -> (b k t) f", f=P)
                          .rearrange("(r p) f -> p r f", p=P)).then_inc(params_loaded, 16)
            act.dma_start(ssrow[:], ins["state_short_conv"][0].rearrange("b k (t f) -> (b k t) f", f=P)
                          .rearrange("(r p) f -> p r f", p=P)).then_inc(params_loaded, 16)
            with nc.allow_non_contiguous_dma(reason="a few columns of one value per head"):
                act.dma_start(hvec[:, 0:1], ins["ssm_dt_bias"][0].rearrange("(h a) -> h a", a=1)).then_inc(cols_loaded, 16)
                act.dma_start(hvec[:, 1:2], ins["ssm_a_log"][0].rearrange("(h a) -> h a", a=1)).then_inc(cols_loaded, 16)
                for half in range(2):
                    d_half = ins["ssm_d"].rearrange("a (q two) -> two a q", two=2)[half]
                    act.dma_start(dcol[half * HD:half * HD + HD, :],
                                  d_half.broadcast_to([HD, HEADS // 2])).then_inc(cols_loaded, 16)

            def split_hi(seg, it, step, pos):
                for slot, n, p_ in split_steps(seg, it, step, pos):
                    wait(act, raw_loaded[slot], raw_count(seg, it, p_))
                    wait(act, multiplied, n - RING + 1)
                    activate(whi[slot][:], raw[slot][:], copy).then_inc(hi_split, 1)

            def load_pair(g, q):
                row = (HPG * g + 2 * q) * HD
                act.dma_start(h0[q % 2][:], ins["state_ssm"][0].rearrange("b h p n -> (h p) b n")[at(row, P)]
                              ).then_inc(h0_loaded[q % 2], 16)

            def rms(n):
                if n == 1:
                    for h in range(4):
                        wait(act, x_kept_v, 2 * h + 2)
                        wait(act, x_kept_a, 2 * h + 2)
                        wait(act, sq_summed, h - 1)
                        activate(sq0[:, h % 2], xt0[:, 4 * h:4 * h + 4, :], ACT.Square).then_inc(sq_ready, 1)
                act.wait_ge(var_ready, n)
                activate(rstd[:], var[:], ACT.Sqrt).then_inc(rstd_ready, 1)
                if n in (2, 3):
                    keep_ple(2 * n - 3)
                if n == 4:
                    return
                for h in range(4):
                    act.wait_ge(n_full, 4 * (n - 1) + h + 1)
                    activate(n_hi[:, 4 * h:4 * h + 4, :], (nt0 if n == 1 else nt)[:, h % 2], copy
                             ).then_inc(n_hi_ready, 1)

            def squares(n, i):
                act.wait_ge(out_added, OUTS_BEFORE[n] - 8 + i + 1)
                if i == 0:
                    act.wait_ge(sq_summed, SUMS[n - 1])
                if i >= 3:
                    act.wait_ge(sq_added, ADDED[n] + i - 2)
                dst = sq_sum if i == 0 else sq_pair[i % 2]
                activate(dst, xt[:, 2 * i:2 * i + 2, :], ACT.Square).then_inc(sq_ready, 1)

            def last_squares(it, half):
                i = 2 * it + half
                act.wait_ge(ple_added, 2 * i + 2)
                act.wait_ge(sq_added, ADDED[4] + i)
                activate(sq_pair[half], xt[:, at(i, 1, 2)], ACT.Square).then_inc(sq_ready, 1)

            def keep_ple(k):
                act.wait_ge(multiplied, PLE_PIECES[k] + 1)
                activate(acc_a[:, 4 * k:4 * k + 4, :], ps[:, 4 * (k % 2):4 * (k % 2) + 4, 0:NT], copy
                         ).then_inc(ple_kept, 1)

            def fin(seg, it, j, outs_end):
                tile_n = 4 * (seg.chunk0 + it) + j
                act.wait_ge(f_ready, tile_n + 1)
                if outs_end is not None:
                    act.wait_ge(multiplied, pw(seg, it, outs_end))
                activate(c_hi[:, j, :], chunk[:, j, :], copy).then_inc(c_hi_ready, 1)

            def silu_x(g, i):
                act.wait_ge(conv_done, 6 * g + i + 1)
                wait(act, yg_ready, 4 * (g - 1) + (i + 1 if i < 4 else 4))
                dst = xs[:, i, :] if i < 4 else bc[:, i - 4, :]
                activate(dst[:, 0:SEQ], prompt_of(cv[:, i % 2], K_X), ACT.Silu)
                activate(dst[:, SEQ:NT].rearrange("p (b l) -> p b l", l=LB), samples_of(cv[:, i % 2], K_X),
                         ACT.Silu).then_inc(xs_ready, 1)

            def tasks(seg, it, step, pos, outs_end):
                kind, j = step[0], step[-1]
                g = it if seg.name == "ssm" else GROUPS
                if kind == "start":
                    for k in range(0, KM, 2):
                        act.wait_ge(x_turned, k + 1)
                        activate(xt0[:, k, :], ps[:, k % 8, 0:NT], copy).then_inc(x_kept_a, 1)
                    act.wait_ge(x_kept_v, 8)
                    act.wait_ge(x_kept_a, 8)
                    act.dma_start(scratch, xt0[:]).then_inc(x_saved, 16)
                    rms(1)
                    for n in range(AHEAD):
                        act.wait_ge(raw_loaded[n], 16)
                        activate(whi[n][:], raw[n][:], copy).then_inc(hi_split, 1)
                elif kind == "out" and seg.name == "mixend":
                    if j == 0:
                        act.wait_ge(f_ready, 4 * C_F)
                        act.dma_start(fsrow[:, 0:5, :], ffn_past[0:5 * P].rearrange("(r p) f -> p r f", p=P)
                                      ).then_inc(ftab_loaded, 16)
                        act.dma_start(fsrow[0:64, 5, :], ffn_past[5 * P:5 * P + 64]).then_inc(ftab_loaded, 16)
                        act.dma_start(perow[:, 0:2, :], ins["p_prompt"][0, 0].rearrange("(c p) f -> p c f", p=P)
                                      ).then_inc(pe_loaded, 16)
                        act.dma_start(perow[0:NS, 2, :], ins["p_sample"][0].rearrange("b l f -> (b l) f")
                                      ).then_inc(pe_loaded, 16)
                    if j == 5:
                        act.wait_ge(pe_kept, 1)
                        activate(peT_hi[:], pef, copy).then_inc(pe_hi, 1)
                    squares(2, j)
                elif kind == "out" and seg.name == "ffnend":
                    if j < len(TAIL_FOURS):
                        act.wait_ge(tail_turned, j + 1)
                        bank, blocks = TAIL_FOURS[j]
                        for m, rows in blocks:
                            activate(trow[0:rows, m, :], ps[0:rows, bank, (m % 4) * P:(m % 4) * P + P], copy
                                     ).then_inc(tail_kept, 1)
                    if j == 6:
                        act.wait_ge(tail_kept, N_TAIL_BLOCKS)
                        for dst, src in tail_stores():
                            act.dma_start(dst, src).then_inc(tails_stored, 16)
                    squares(3, j)
                elif kind == "rms":
                    rms(j)
                elif kind == "unit" and step[1] == "dt":
                    act.wait_ge(dt_min, 1)
                    activate(wm[0:HEADS, 2, 0:NT], wm[0:HEADS, 1, 0:NT], ACT.Exp).then_inc(dt_exp, 1)
                    act.wait_ge(cols_loaded, 16 * 4)
                    activate(hvec[:, 2:3], hvec[:, 1:2], ACT.Exp).then_inc(a_exp, 1)
                elif kind == "dtab":
                    act.wait_ge(dt_sums, 1)
                    activate(heads_tab[:, :, 3:5, :].rearrange("p g c h -> p c g h"),
                             ps[:, 5, 0:2 * HEADS].rearrange("p (c g h) -> p c g h", c=2, g=GROUPS), ACT.Exp)
                    activate(heads_tab[0:NS, :, 5, :],
                             ps[0:NS, 5, 2 * HEADS:3 * HEADS].rearrange("p (g h) -> p g h", g=GROUPS), ACT.Exp)
                    activate(heads_tab[:, :, 12, :],
                             ps[:, 6, 0:HEADS].rearrange("p (g h) -> p g h", g=GROUPS), ACT.Exp).then_inc(dt_decay, 1)
                elif kind == "unit" and step[1] == "x":
                    act.wait_ge(multiplied, pw(seg, it, pos + 1))
                    wait(act, conv_done, 6 * g + j - 1)
                    wait(act, xtail_kept, 6 * g + j - 1)
                    if seg.start == 0 and j == 0:
                        act.wait_ge(x_saved, 16)
                    if j == 0:
                        load_pair(g, 0)
                        load_pair(g, 1)
                    unit_ps = ps[:, j % 2, :]
                    activate(prompt_of(xpad[j % 2], K_X, K_X - 1), unit_ps[:, 0:SEQ], copy)
                    activate(samples_of(xpad[j % 2], K_X, K_X - 1),
                             unit_ps[:, SEQ:NT].rearrange("p (b l) -> p b l", l=LB), copy).then_inc(xpad_filled, 1)
                    if j:
                        silu_x(g, j - 1)
                elif kind == "unit" and step[1] == "z":
                    if j == 0:
                        silu_x(g, 5)
                        wait(act, vs_done, g)
                    act.wait_ge(multiplied, pw(seg, it, pos + 1))
                    activate(zs[:, j, :], ps[:, j % 2, 0:NT], ACT.Silu).then_inc(z_ready, 1)
                elif kind == "ssd1":
                    act.wait_ge(bt_done, g + 1)
                    activate(bt[:, 0:2, :], ps[:, 5, 0:2 * P].rearrange("p (c n) -> p c n", n=P), copy)
                    activate(bt[0:NS, 2, :], ps[0:NS, 5, 2 * P:3 * P], copy).then_inc(bt_kept, 1)
                elif kind == "ssd2":
                    for quad in range(5):
                        act.wait_ge(q_min, 5 * g + quad + 1)
                        part = wm[:, quad, :] if quad < 4 else wm[0:NS, quad, :]
                        activate(part, part, ACT.Exp).then_inc(q_exp, 1)
                    wait(act, hd_done, 8 * g)
                    for half in range(2):
                        act.wait_ge(ea_done, 2 * g + half + 1)
                        activate(ea[:, 2 * half:2 * half + 2, :],
                                 ps[:, 6 + half, 0:2 * (P + NS + NB)].rearrange("p (q n) -> p q n", q=2),
                                 ACT.Exp).then_inc(ea_exp, 1)
                elif kind == "ssd3":
                    act.wait_ge(h1_done, 2 * g + 1)
                    activate(h1t[:], ps[:, 2, :], copy).then_inc(h1_kept, 1)
                    act.wait_ge(h1_done, 2 * g + 2)
                    wait(act, hfin_stored, 16 * g)
                    activate(hfin[:].rearrange("p q n -> p (q n)"), ps[:, 3, :], copy).then_inc(h1_kept, 1)
                    act.wait_ge(h1_kept, 2 * g + 2)
                    act.dma_start(outs["ssm_prompt"][0, 0].rearrange("h p n -> (h p) n")
                                  .rearrange("(q m) n -> m q n", m=P)[:, at(4 * g, 4)],
                                  hfin[:]).then_inc(hfin_stored, 16)
                elif kind == "pair":
                    wait(act, yoff_done, 4 * g + j)
                    for half in range(2):
                        act.wait_ge(t_done, 8 * g + 2 * j + half + 1)
                        activate(h0t[:, 4 * half:4 * half + 4, :].rearrange("p b n -> p (b n)"),
                                 ps[:, 4 + half, :], copy).then_inc(t_kept, 1)
                    act.wait_ge(yg_ready, 4 * g + j + 1)
                    activate(zs[:, j, :], chunk[:, j, :], ACT.Square).then_inc(ysq_ready, 1)
                    act.wait_ge(hd_done, 8 * g + 2 * j + 2)
                    if j < 2:
                        load_pair(g, j + 2)
                    act.wait_ge(hn_added, 8 * g + 2 * j + 2)
                    act.dma_start(outs["ssm_sample"][0].rearrange("b h p n -> (h p) b n")[at((HPG * g + 2 * j) * HD, P)],
                                  hn[j % 2][:]).then_inc(hn_stored[j % 2], 16)
                elif kind == "norm":
                    act.wait_ge(vinv, g)
                    activate(rstd[:], var[:], ACT.Sqrt).then_inc(yrstd, 1)
                    for q in range(4):
                        act.wait_ge(f_ready, 4 * (g - 1) + q + 1)
                        activate(c_hi[:, q, :], chunk[:, q, :], copy).then_inc(c_hi_ready, 1)
                    if seg.name == "sc":
                        ssm_over(act)
                        act.dma_start(xt[:], scratch).then_inc(x_back, 16)
                elif kind == "unit" and step[1] == "c":
                    t = 4 * it + j
                    if seg.start == 0 and j == 0:
                        ssm_over(act)
                    act.wait_ge(multiplied, pw(seg, it, pos + 1))
                    wait(act, prod_done, t - 1)
                    activate(cmul[:, j % 2, :], ps[:, (3 * j) % 4, 0:NT], copy).then_inc(cmul_ready, 1)
                elif kind == "unit" and step[1] in ("ga", "gb"):
                    if seg.loop or j >= 2:
                        act.wait_ge(f_ready, 4 * (C_MIX + it) + j - 1)
                    act.wait_ge(multiplied, pw(seg, it, pos + 1))
                    which, bank = (sig_a, 2 * j) if step[1] == "ga" else (sig_b, 2 * j + 1)
                    activate(which[:, j % 2, :], ps[:, bank % 4, 0:NT], ACT.Sigmoid).then_inc(sigs, 1)
                elif kind == "unit" and step[1] == "g":
                    act.wait_ge(multiplied, pw(seg, it, pos + 1))
                    act.wait_ge(sconv_done, 16 + 4 * it + j - 1)
                    act.wait_ge(stail_kept, 16 + 4 * it + j - 1)
                    unit_ps = ps[:, (2 * j) % 4, :]
                    activate(prompt_of(spad[j % 2], K_F, K_F - 1), unit_ps[:, 0:SEQ], copy)
                    activate(samples_of(spad[j % 2], K_F, K_F - 1),
                             unit_ps[:, SEQ:NT].rearrange("p (b l) -> p b l", l=LB), copy).then_inc(spad_filled, 1)
                elif kind == "unit" and step[1] == "u":
                    act.wait_ge(sconv_done, 16 + 4 * it + j + 1)
                    act.wait_ge(f_ready, 4 * (C_F + it) + j - 1)
                    gact = sig_a[:, j % 2, :]
                    activate(gact[:, 0:SEQ], prompt_of(scv[:, j % 2, :], K_F), ACT.Silu)
                    activate(gact[:, SEQ:NT].rearrange("p (b l) -> p b l", l=LB),
                             samples_of(scv[:, j % 2, :], K_F), ACT.Silu).then_inc(gact_ready, 1)
                elif kind == "fin":
                    fin(seg, it, j, outs_end)
                elif kind == "ple" and j % 2 == 0:
                    keep_ple(j)
                elif kind == "unit" and step[1] == "pg":
                    act.wait_ge(multiplied, pw(seg, it, pos + 1))
                    wait(act, ple_added, 4 * it + j - 1) if seg.start or j >= 2 else None
                    activate(sig_a[:, j % 2, :], ps[:, j, 0:NT], ACT.Sigmoid).then_inc(sigs, 1)
                    if j % 2:
                        last_squares(it, j // 2)
                elif kind == "end":
                    for c in range(3):
                        rows = P if c < 2 else NS
                        if c == 2:
                            act.wait_ge(tails_stored, 16 * len(list(tail_stores())))
                        act.wait_ge(y_turned, 4 * c + 2)
                        b0 = 4 * (c % 2)
                        activate(yrow[c][0:rows, 0:DM // 2].rearrange("p (b n) -> p b n", n=512),
                                 ps[0:rows, b0:b0 + 2, :], copy).then_inc(y_kept_a, 1)
                        act.wait_ge(y_kept_a, c + 1)
                        act.wait_ge(y_kept_v, c + 1)
                        dst = (outs["y_prompt"][0, c * P:(c + 1) * P, :] if c < 2
                               else outs["y_sample"].rearrange("b l d -> (b l) d"))
                        act.dma_start(dst, yrow[c][0:rows, :]).then_inc(y_stored, 16)

            def visit(seg, it):
                run_steps(act, seg, it, split_hi, tasks)
            walk(act, visit)

        @block.vector
        def _(dve):
            own = Own(dve, dve_own)
            v = nc.vector
            tt, ts, stt = v.tensor_tensor, v.tensor_scalar, v.scalar_tensor_tensor
            MUL, ADD, SUB = ALU.mult, ALU.add, ALU.subtract

            def split_lo(seg, it, step, pos):
                for slot, n, p_ in split_steps(seg, it, step, pos):
                    dve.wait_ge(hi_split, n + 1)
                    tt(wlo[slot][:], raw[slot][:], whi[slot][:].bitcast(F32), SUB).then_inc(lo_split, 1)

            def mean_square(n):
                dve.wait_ge(sq_summed, SUMS[n])
                own(ts(var[:], ps[:, RMS_BANK[n], 0:NT], 1.0 / DM, EPS, MUL, ADD))
                v.reciprocal(var[:], var[:]).then_inc(var_ready, 1)

            def rms(n):
                src, full = (xt0, nt0) if n == 1 else (xt, nt)
                gain = PARAMS[f"g{n}"][0]
                if n == 4:
                    dve.wait_ge(ple_added, KM)
                dve.wait_ge(rstd_ready, n)

                def gained(h):
                    if n < 4:
                        wait(dve, n_ready, 4 * (n - 1) + h - 1)
                    for q in range(4):
                        k = 4 * h + q
                        dst = acc_a[:, k, :] if n == 4 else full[:, h % 2, q, :]
                        last = stt(dst, src[:, k, :], ptab[:, gain + k:gain + k + 1], rstd[:], MUL, MUL)
                    last.then_inc(y_full if n == 4 else n_full, 1)

                def lower(h):
                    dve.wait_ge(n_hi_ready, 4 * (n - 1) + h + 1)
                    tt(n_lo[:, 4 * h:4 * h + 4, :], full[:, h % 2], n_hi[:, 4 * h:4 * h + 4, :].bitcast(F32),
                       SUB).then_inc(n_ready, 1)

                for h in range(4):
                    gained(h)
                    if n < 4 and h:
                        lower(h - 1)
                if n < 4:
                    lower(3)

            def fin(seg, it, j):
                dve.wait_ge(c_hi_ready, 4 * (seg.chunk0 + it) + j + 1)
                tt(c_lo[:, j, :], chunk[:, j, :], c_hi[:, j, :].bitcast(F32), SUB).then_inc(c_ready, 1)

            def taps(dst, pad, weights, bias, n):
                own(ts(dst, pad[:, 0:n], weights[0], bias, MUL, ADD) if bias is not None
                    else ts(dst, pad[:, 0:n], weights[0], None, MUL))
                for k in range(1, len(weights) - 1):
                    own(stt(dst, pad[:, k:k + n], weights[k], dst, MUL, ADD))
                k = len(weights) - 1
                return stt(dst, pad[:, k:k + n], weights[k], dst, MUL, ADD)

            def xchunk(dst, c, heads, rows):
                return tt(dst.rearrange("p (h d) -> p h d", d=HD),
                          ps[0:rows, 2 + c, :].rearrange("p (h d) -> p h d", d=HD),
                          heads.unsqueeze(2).broadcast_to([rows, HPG, HD]), MUL)

            def quad_min(g, quad):
                dve.wait_ge(q_done, 5 * g + quad + 1)
                c, bank = QUADS[quad]
                rows, width, n = (P, P, 4) if quad < 4 else (NS, NS, 8)
                for i in range(n):
                    h = (4 * (quad % 2) if quad < 4 else 0) + i
                    last = ts(wm[0:rows, quad, i * width:(i + 1) * width],
                              ps[0:rows, bank, i * width:(i + 1) * width],
                              hcol[0:rows, 6 + c, h:h + 1], 0.0, SUB, ALU.min)
                last.then_inc(q_min, 1)

            def tasks(seg, it, step, pos, outs_end):
                kind, j = step[0], step[-1]
                g = it if seg.name == "ssm" else GROUPS
                if kind == "start":
                    for k in range(1, KM, 2):
                        dve.wait_ge(x_turned, k + 1)
                        v.tensor_copy(xt0[:, k, :], ps[:, k % 8, 0:NT]).then_inc(x_kept_v, 1)
                    for n, (dst, rows_of) in enumerate(TAB_COPIES):
                        dve.wait_ge(tab_turned, n + 1)
                        v.tensor_copy(dst, ps[:, TAB_BANKS[n], 0:rows_of]).then_inc(tab_kept, 1)
                    dve.wait_ge(tab_kept, len(TAB_COPIES))
                    dve.wait_ge(x_kept_v, KM // 2)
                    dve.wait_ge(x_kept_a, KM // 2)
                    mean_square(1)
                    rms(1)
                    for n in range(AHEAD):
                        dve.wait_ge(hi_split, n + 1)
                        tt(wlo[n][:], raw[n][:], whi[n][:].bitcast(F32), SUB).then_inc(lo_split, 1)
                elif kind == "rsum":
                    mean_square(j)
                elif kind == "rms":
                    rms(j)
                elif kind == "unit" and step[1] == "dt":
                    w = [wm[0:HEADS, i, 0:NT] for i in range(5)]
                    dve.wait_ge(multiplied, pw(seg, it, pos + 1))
                    dve.wait_ge(cols_loaded, 16 * 4)
                    dve.wait_ge(x_saved, 16)
                    own(ts(w[0], ps[0:HEADS, DT_BANK, 0:NT], hvec[:, 0:1], None, ADD))
                    stt(w[1], w[0], -1.0, w[0], MUL, ALU.min).then_inc(dt_min, 1)
                    dve.wait_ge(dt_exp, 1)
                    own(ts(w[3], w[2], 2.0, None, ADD))
                    own(v.reciprocal(w[3], w[3]))
                    own(tt(w[3], w[2], w[3], MUL))
                    own(tt(w[4], w[3], w[3], MUL))
                    own(ts(w[1], w[4], 1.0 / 15, None, MUL))
                    for n in (13, 11, 9, 7, 5, 3):
                        own(stt(w[1], w[1], 1.0 / n, w[4], ADD, MUL))
                    own(stt(w[1], w[1], 1.0, w[3], ADD, MUL))
                    own(ts(w[2], w[0], 0.0, None, ALU.max))
                    own(stt(w[0], w[1], 2.0, w[2], MUL, ADD))
                    dve.wait_ge(a_exp, 1)
                    ts(w[1], w[0], hvec[:, 2:3], -1.0, MUL, MUL).then_inc(dt_done, 1)
                elif kind == "dtab":
                    dve.wait_ge(consts_ready, N_CONSTS)
                    dve.wait_ge(dt_turned, 1)

                    def keep(kc, bank):
                        v.tensor_copy(heads_tab[:, :, kc:kc + 2, :].rearrange("p g c h -> p c g h"),
                                      ps[:, bank, 0:2 * HEADS].rearrange("p (c g h) -> p c g h", c=2, g=GROUPS))
                        return v.tensor_copy(heads_tab[0:NS, :, kc + 2, :],
                                             ps[0:NS, bank, 2 * HEADS:3 * HEADS].rearrange("p (g h) -> p g h", g=GROUPS))
                    keep(0, 2)
                    keep(9, 3).then_inc(a_kept, 1)
                    dve.wait_ge(dt_sums, 1)
                    keep(6, 4)
                    dve.wait_ge(dt_decay, 1)
                    for c in range(2):
                        tt(heads_tab[:, :, 3 + c, :], heads_tab[:, :, 3 + c, :], heads_tab[:, :, c, :], MUL)
                    tt(heads_tab[0:NS, :, 5, :], heads_tab[0:NS, :, 5, :], heads_tab[0:NS, :, 2, :], MUL)
                    tt(heads_tab[:, :, 12, :], heads_tab[:, :, 12, :], heads_tab[:, :, 0, :], MUL
                       ).then_inc(heads_ready, 1)
                elif kind == "unit" and step[1] == "x":
                    dve.wait_ge(xpad_filled, 6 * g + j + 1)
                    dve.wait_ge(xpast, 6 * g + j + 1)
                    dve.wait_ge(gcol_ready, g + 1)
                    wait(dve, xs_ready, 6 * g + j - 1)
                    taps(cv[:, j % 2, 0:N_CX], xpad[j % 2], [gcol[:, k, j:j + 1] for k in range(K_X)],
                         gcol[:, K_X, j:j + 1], N_CX).then_inc(conv_done, 1)
                elif kind == "ssd1":
                    dve.wait_ge(hcol_ready, g + 1)
                    for c in range(3):
                        rows = P if c < 2 else NS
                        dve.wait_ge(xt_done, 3 * g + c + 1)
                        xchunk(xdt[0:rows, c, :], c, hcol[0:rows, c, :], rows)
                        if c == 0:
                            xchunk(xwf[:], c, hcol[:, 12, :], rows)
                        xchunk(xwe[0:rows, c, :], c, hcol[0:rows, 3 + c, :], rows).then_inc(xw_ready, 1)
                    dve.wait_ge(cb_done, g + 1)
                    tt(cbm[:, 0:2, :], ps[:, 6, 0:2 * P].rearrange("p (c n) -> p c n", c=2),
                       tri[:].unsqueeze(1).broadcast_to([P, 2, P]), MUL)
                    tt(cbm[0:NS, 2, 0:NS], ps[0:NS, 6, 2 * P:2 * P + NS], tri_s[:, 0:NS], MUL).then_inc(cbm_ready, 1)
                    quad_min(g, 0)
                    dve.wait_ge(bt_kept, g + 1)
                    tt(bblk[:], bt[0:NS, 2, :].unsqueeze(1).broadcast_to([NS, NB, P]),
                       tri_s[:, NS:NS + NB].unsqueeze(2).broadcast_to([NS, NB, P]), MUL).then_inc(bblk_ready, 1)
                elif kind == "ssd2":
                    for quad in range(1, 5):
                        quad_min(g, quad)
                    dve.wait_ge(cbm_ready, g + 1)
                    for quad in range(5):
                        dve.wait_ge(q_exp, 5 * g + quad + 1)
                        c = QUADS[quad][0]
                        rows, n = (P, 4) if quad < 4 else (NS, 8)
                        w3 = wm[0:rows, quad, :].rearrange("p (h n) -> p h n", h=n)
                        width = 512 // n
                        tt(w3, w3, cbm[0:rows, c, 0:width].unsqueeze(1).broadcast_to([rows, n, width]), MUL
                           ).then_inc(w_ready, 1)
                elif kind == "pair":
                    y = chunk[:, j, :]
                    dve.wait_ge(yd_done, 4 * g + j + 1)
                    dve.wait_ge(ea_exp, 2 * g + j // 2 + 1)
                    dve.wait_ge(z_ready, 4 * g + j + 1)
                    own(stt(y, xs[:, j, :], gd[:, j:j + 1], ps[:, 6, 0:NT], MUL, ADD))
                    for half in range(2):
                        dve.wait_ge(hn_done, 8 * g + 2 * j + half + 1)
                        dve.wait_ge(hd_done, 8 * g + 2 * j + half + 1)
                        hh = hn[j % 2][:, 4 * half:4 * half + 4, :].rearrange("p b n -> p (b n)")
                        tt(hh, hh, ps[:, HN_BANKS[half], :], ADD).then_inc(hn_added, 1)
                    dve.wait_ge(yoff_done, 4 * g + j + 1)
                    own(tt(yoffs[:], ps[:, 3, 0:P + NS], ea[:, j, 0:P + NS], MUL))
                    own(tt(y[:, P:NT], y[:, P:NT], yoffs[:], ADD))
                    tt(y, y, zs[:, j, :], MUL).then_inc(yg_ready, 1)
                elif kind == "norm":
                    dve.wait_ge(vs_done, g)
                    ts(var[:], ps[:, VS_BANK, 0:NT], GROUPS / DI, EPS, MUL, ADD).then_inc(vsum_read, 1)
                    dve.wait_ge(vsum_read, g)
                    v.reciprocal(var[:], var[:]).then_inc(vinv, 1)
                    dve.wait_ge(yrstd, g)
                    dve.wait_ge(gnrm_ready, g)
                    for q in range(4):
                        stt(chunk[:, q, :], chunk[:, q, :], gnrm[:, q:q + 1], rstd[:], MUL, MUL).then_inc(f_ready, 1)
                    for q in range(4):
                        dve.wait_ge(c_hi_ready, 4 * (g - 1) + q + 1)
                        tt(c_lo[:, q, :], chunk[:, q, :], c_hi[:, q, :].bitcast(F32), SUB).then_inc(c_ready, 1)
                    if seg.name == "sc":
                        ssm_over(dve)
                        v.memset(acc_b[:], 0.0).then_inc(post_zero, 1)
                elif kind == "out":
                    dve.wait_ge(multiplied, pw(seg, it, pos))
                    acc = {"ssm": acc_a, "sc": acc_b, "mix": xt, "ffn": xt}[seg.outs]
                    if seg.outs == "ssm" and j == 0:
                        dve.wait_ge(consts_ready, N_CONSTS)
                    if seg.outs == "sc" and j == 0:
                        dve.wait_ge(post_zero, 1)
                    if seg.outs == "mix" and j == 0:
                        dve.wait_ge(x_back, 16)
                    b0 = OUT_BANKS[j % 2]
                    dst = acc[:, 2 * j:2 * j + 2, :]
                    tt(dst, dst, ps[:, b0:b0 + 2, 0:NT], ADD).then_inc(out_added, 1)
                    if seg.name == "mixend" and j == 3:
                        for n in range(2):
                            dve.wait_ge(ftab_turned, n + 1)
                            lo, hi = 4 * P * n, min(4 * P * (n + 1), NB * (K_F - 1) * (DFF // P))
                            v.tensor_copy(fstate[:].rearrange("p r t -> p (r t)")[:, lo:hi],
                                          ps[:, 2 + n, 0:hi - lo]).then_inc(ftab_kept, 1)
                    if seg.name == "mixend" and j == 4:
                        dve.wait_ge(pe_turned, 1)
                        v.tensor_copy(pef, ps[:, 0:2, 0:NT]).then_inc(pe_kept, 1)
                    if seg.name == "mixend" and j == 5:
                        dve.wait_ge(pe_hi, 1)
                        tt(peT_lo[:], pef, peT_hi[:].bitcast(F32), SUB).then_inc(pe_ready, 1)
                elif kind == "unit" and step[1] == "h":
                    t = 4 * it + j
                    dve.wait_ge(multiplied, pw(seg, it, pos + 1))
                    dve.wait_ge(cmul_ready, t + 1)
                    wait(dve, sconv_done, t - 1) if seg.loop or j >= 2 else None
                    wait(dve, stail_kept, t - 1) if seg.loop or j >= 2 else None
                    h_ps = ps[:, (3 * j + 1) % 4, :]
                    tt(prompt_of(spad[j % 2], K_SC, K_SC - 1), h_ps[:, 0:SEQ], cmul[:, j % 2, 0:SEQ], MUL)
                    tt(samples_of(spad[j % 2], K_SC, K_SC - 1),
                       h_ps[:, SEQ:NT].rearrange("p (b l) -> p b l", l=LB),
                       cmul[:, j % 2, SEQ:NT].rearrange("p (b l) -> p b l", l=LB), MUL).then_inc(prod_done, 1)
                    dve.wait_ge(prod_done, t + 1)
                    dve.wait_ge(spast, t + 1)
                    dve.wait_ge(gcol_ready, 8 + it + 1)
                    taps(scv[:, j % 2, 0:N_CS], spad[j % 2], [scol[:, k, j:j + 1] for k in range(K_SC)],
                         None, N_CS).then_inc(sconv_done, 1)
                elif kind == "unit" and step[1] == "b":
                    t = 4 * it + j
                    dve.wait_ge(multiplied, pw(seg, it, pos + 1))
                    dve.wait_ge(sconv_done, t + 1)
                    b_ps = ps[:, (3 * j + 2) % 4, :]
                    f = chunk[:, j, :]
                    tt(f[:, 0:SEQ], b_ps[:, 0:SEQ], prompt_of(scv[:, j % 2, :], K_SC), MUL)
                    tt(f[:, SEQ:NT].rearrange("p (b l) -> p b l", l=LB),
                       b_ps[:, SEQ:NT].rearrange("p (b l) -> p b l", l=LB),
                       samples_of(scv[:, j % 2, :], K_SC), MUL).then_inc(f_ready, 1)
                elif kind == "mix":
                    t = 4 * it + j
                    dve.wait_ge(sigs, 2 * t + 2)
                    dve.wait_ge(out_added, 8 * C_MIX)
                    ga, gb = sig_a[:, j % 2, :], sig_b[:, j % 2, :]
                    tt(ga, ga, acc_a[:, at(t)].rearrange("p a n -> p (a n)"), MUL)
                    own(tt(gb, gb, acc_b[:, at(t)].rearrange("p a n -> p (a n)"), MUL))
                    tt(chunk[:, j, :], ga, gb, ADD).then_inc(f_ready, 1)
                elif kind == "unit" and step[1] == "g":
                    dve.wait_ge(spad_filled, 4 * it + j + 1)
                    dve.wait_ge(spast, 16 + 4 * it + j + 1)
                    dve.wait_ge(gcol_ready, 12 + it + 1)
                    if seg.loop or j >= 2:
                        dve.wait_ge(gact_ready, 4 * it + j - 1)
                    taps(scv[:, j % 2, 0:N_CS], spad[j % 2], [scol[:, k, j:j + 1] for k in range(K_F)],
                         scol[:, K_F, j:j + 1], N_CS).then_inc(sconv_done, 1)
                elif kind == "unit" and step[1] == "u":
                    dve.wait_ge(multiplied, pw(seg, it, pos + 1))
                    dve.wait_ge(gact_ready, 4 * it + j + 1)
                    tt(chunk[:, j, :], ps[:, (2 * j + 1) % 4, 0:NT], sig_a[:, j % 2, :], MUL).then_inc(f_ready, 1)
                elif kind == "fin":
                    fin(seg, it, j)
                elif kind == "unit" and step[1] == "pg":
                    dve.wait_ge(sigs, 32 + 4 * it + j + 1)
                    dve.wait_ge(ple_kept, 4)
                    ga = sig_a[:, j % 2, :]
                    own(tt(ga, ga, acc_a[:, at(4 * it + j)].rearrange("p a n -> p (a n)"), MUL))
                    dst = xt[:, at(4 * it + j)].rearrange("p a n -> p (a n)")
                    tt(dst, dst, ga, ADD).then_inc(ple_added, 1)
                elif kind == "end":
                    for c in range(3):
                        rows = P if c < 2 else NS
                        if c == 2:
                            dve.wait_ge(tails_stored, 16 * len(list(tail_stores())))
                        dve.wait_ge(y_turned, 4 * c + 4)
                        b0 = 4 * (c % 2) + 2
                        v.tensor_copy(yrow[c][0:rows, DM // 2:DM].rearrange("p (b n) -> p b n", n=512),
                                      ps[0:rows, b0:b0 + 2, :]).then_inc(y_kept_v, 1)

            def visit(seg, it):
                run_steps(dve, seg, it, split_lo, tasks)
            walk(dve, visit, own, DVE_LINKS)

        @block.gpsimd
        def _(pool):
            g_ = nc.gpsimd
            g_.memset(acc_a[:], 0.0).then_inc(consts_ready, 1)
            g_.memset(heads_tab[:], 0.0).then_inc(consts_ready, 1)
            for m in (ident, ones, tri, after, tri_s, after_s):
                g_.memset(m[:], 0.0 if m is ident else 1.0).then_inc(consts_ready, 1)
            pool.wait_ge(consts_ready, 8)
            g_.affine_select(out=ident[:], in_=ident[:], compare_op=ALU.not_equal, fill=1.0, base=0,
                             pattern=[[-1, P]], channel_multiplier=1).then_inc(consts_ready, 1)
            g_.affine_select(out=tri[:], in_=tri[:], compare_op=ALU.is_ge, fill=0.0, base=0,
                             pattern=[[1, P]], channel_multiplier=-1).then_inc(consts_ready, 1)
            g_.affine_select(out=after[:], in_=after[:], compare_op=ALU.is_gt, fill=0.0, base=0,
                             pattern=[[-1, P]], channel_multiplier=1).then_inc(consts_ready, 1)
            own = Own(pool, pool_own)
            same, last8 = tri_s[:, 0:NS].rearrange("p (b l) -> p b l", l=LB), tri_s[:, NS:NS + NB]
            for m3 in (same, after_s[:].rearrange("p (b l) -> p b l", l=LB)):
                own(g_.affine_select(out=m3, in_=m3, compare_op=ALU.is_ge, fill=0.0, base=0,
                                     pattern=[[-LB, NB], [0, LB]], channel_multiplier=1))
                own(g_.affine_select(out=m3, in_=m3, compare_op=ALU.is_ge, fill=0.0, base=LB - 1,
                                     pattern=[[LB, NB], [0, LB]], channel_multiplier=-1))
            own(g_.affine_select(out=last8, in_=last8, compare_op=ALU.is_ge, fill=0.0, base=0,
                                 pattern=[[-LB, NB]], channel_multiplier=1))
            own(g_.affine_select(out=last8, in_=last8, compare_op=ALU.is_ge, fill=0.0, base=LB - 1,
                                 pattern=[[LB, NB]], channel_multiplier=-1))
            own(g_.affine_select(out=tri_s[:, 0:NS], in_=tri_s[:, 0:NS], compare_op=ALU.is_ge, fill=0.0, base=0,
                                 pattern=[[1, NS]], channel_multiplier=-1))
            g_.affine_select(out=after_s[:], in_=after_s[:], compare_op=ALU.is_gt, fill=0.0, base=0,
                             pattern=[[-1, NS]], channel_multiplier=1).then_inc(consts_ready, 1)

            def past_and_last(pad, taps, state, tail, t, filled, past, kept, j, tile_n, before):
                wait(pool, before, tile_n - 1)
                g_.tensor_copy(samples_of(pad, taps, 0, taps - 1),
                               state[:, :, at(t)].rearrange("p (b k) a -> p b (k a)", b=NB)).then_inc(past, 1)
                pool.wait_ge(filled[0], filled[1])
                pool.wait_ge(past, tile_n + 1)
                g_.tensor_copy(tail[:, :, :, at(t)].rearrange("p i k a -> p i (k a)"),
                               last_rows(pad, taps)).then_inc(kept, 1)

            def tasks(seg, it, step):
                kind, j = step[0], step[-1]
                g = it if seg.name == "ssm" else GROUPS
                if kind == "unit" and step[1] == "x":
                    if j == 0:
                        if seg.start == 0:
                            pool.wait_ge(x_saved, 16)
                            pool.wait_ge(n_ready, 4)
                            pool.wait_ge(tab_kept, len(TAB_COPIES))
                            for i in range(2):
                                g_.memset(xpad[i][:, 0:K_X - 1], 0.0)
                        wait(pool, conv_done, 6 * g)
                        conv_tab = ptab[:, PARAMS["cx"][0]:PARAMS["cx"][0] + (K_X + 1) * (XBC // P)].rearrange(
                            "p (k t) -> p k t", k=K_X + 1)
                        g_.tensor_copy(gcol[:, :, 0:4], conv_tab[:, :, at(4 * g, 4)])
                        g_.tensor_copy(gcol[:, :, 4:5], conv_tab[:, :, at(DI // P + g)])
                        g_.tensor_copy(gcol[:, :, 5:6], conv_tab[:, :, at(DI // P + GROUPS + g)]
                                       ).then_inc(gcol_ready, 1)
                    t = (4 * g + j) if j < 4 else DI // P + (j - 4) * GROUPS + g
                    past_and_last(xpad[j % 2], K_X, xstate, xtail, t, (xpad_filled, 6 * g + j + 1),
                                  xpast, xtail_kept, j, 6 * g + j, conv_done)
                    if j == 2:
                        wait(pool, yg_ready, 4 * g)
                        if seg.start == 0:
                            pool.wait_ge(heads_ready, 1)
                            pool.wait_ge(cols_loaded, 16 * 4)
                        g_.tensor_copy(gd[:], dcol[:, at(4 * g, 4)])
                        g_.tensor_copy(hcol[:].rearrange("p a b -> p (a b)"),
                                       heads_tab[:, at(g)].rearrange("p a k h -> p (a k h)")).then_inc(hcol_ready, 1)
                elif kind == "ssd1":
                    wait(pool, f_ready, 4 * g)
                    gy = PARAMS["gy"][0]
                    g_.tensor_copy(gnrm[:], ptab[:, at(gy + 4 * g, 4)]).then_inc(gnrm_ready, 1)
                elif kind == "pair":
                    pool.wait_ge(ea_exp, 2 * g + j // 2 + 1)
                    pool.wait_ge(h0_loaded[j % 2], 16 * (2 * g + j // 2 + 1))
                    wait(pool, hn_stored[j % 2], 16 * (2 * g + j // 2))
                    for half in range(2):
                        b = slice(4 * half, 4 * half + 4)
                        g_.tensor_tensor(hn[j % 2][:, b, :], h0[j % 2][:, b, :],
                                         ea[:, j, P + NS + 4 * half:P + NS + 4 * half + 4].unsqueeze(2)
                                         .broadcast_to([P, 4, P]), ALU.mult).then_inc(hd_done, 1)
                    for q in {0: (), 1: (), 2: (1,), 3: (2, 3)}[j]:
                        pool.wait_ge(ysq_ready, 4 * g + q + 1)
                        wait(pool, ysum_ready, 3 * g + q - 1)
                        g_.tensor_tensor(zs[:, 0, :], zs[:, 0, :], zs[:, q, :], ALU.add).then_inc(ysum_ready, 1)
                elif kind == "out":
                    if seg.name in ("mixend", "ffnend") and j:
                        n = 2 if seg.name == "mixend" else 3
                        pool.wait_ge(sq_ready, SQUARES[n] + j + 1)
                        wait(pool, sq_added, ADDED[n] + j - 1)
                        g_.tensor_tensor(sq_sum, sq_sum, sq_pair[j % 2], ALU.add).then_inc(sq_added, 1)
                elif kind == "rms" and j == 3:
                    pool.wait_ge(sq_summed, SUMS[3])
                    g_.memset(sq_sum, 0.0).then_inc(sq_added, 1)
                elif kind == "unit" and step[1] == "pg" and j % 2:
                    i = 2 * it + j // 2
                    pool.wait_ge(sq_ready, SQUARES[4] + i + 1)
                    pool.wait_ge(sq_added, ADDED[4] + 1 + i)
                    g_.tensor_tensor(sq_sum, sq_sum, sq_pair[j // 2], ALU.add).then_inc(sq_added, 1)
                elif kind == "unit" and step[1] == "c":
                    if seg.start == 0 and j == 0:
                        ssm_over(pool)
                        for i in range(2):
                            g_.memset(spad[i][:, 0:K_SC - 1], 0.0)
                    if j == 0:
                        wait(pool, sconv_done, 4 * it)
                        base = PARAMS["cs"][0]
                        g_.tensor_copy(scol[:, 0:K_SC, :], ptab[:, base:base + K_SC * KM].rearrange(
                            "p (k t) -> p k t", k=K_SC)[:, :, at(4 * it, 4)]).then_inc(gcol_ready, 1)
                    past_and_last(spad[j % 2], K_SC, sstate, stail, 4 * it + j, (prod_done, 4 * it + j + 1),
                                  spast, stail_kept, j, 4 * it + j, sconv_done)
                elif kind == "unit" and step[1] == "g":
                    t = 4 * it + j
                    if j == 0:
                        pool.wait_ge(sconv_done, 16 + 4 * it)
                        pool.wait_ge(ftab_kept, 2)
                        base = PARAMS["cf"][0]
                        g_.tensor_copy(scol[:], ptab[:, base:base + (K_F + 1) * (DFF // P)].rearrange(
                            "p (k t) -> p k t", k=K_F + 1)[:, :, at(4 * it, 4)]).then_inc(gcol_ready, 1)
                    past_and_last(spad[j % 2], K_F, fstate, ftail, t, (spad_filled, t + 1),
                                  spast, stail_kept, j, 16 + t, sconv_done)

            def visit(seg, it):
                for step in seg.steps:
                    tasks(seg, it, step)
            for seg in SEGS:
                if seg.name not in ("prologue", "mix", "finish"):
                    if seg.loop:
                        with pool.Fori(seg.start, seg.stop) as it:
                            visit(seg, it)
                    else:
                        visit(seg, seg.start)

        @block.tensor
        def _(pe):
            mm, turn = nc.tensor.matmul, nc.tensor.transpose

            def three(out, w_h, w_l, x_h, x_l, first, last):
                mm(out, w_h, x_h, start=first, stop=False)
                mm(out, w_h, x_l, start=False, stop=False)
                return mm(out, w_l, x_h, start=False, stop=last)

            def piece_ready(seg, it, pos):
                wait(pe, lo_split, first_piece(seg, it) + pos + 1)
                return (seg.piece0 + pos) % RING

            def token_rows(c):
                return slice(c * P, c * P + (P if c < 2 else NS))

            def bank_free(seg, it, step):
                kind, j = step[1], step[-1]
                g = it
                early = seg.start == 0 and j < 2
                if kind == "dt":
                    return DT_BANK
                if kind == "x":
                    if j == 0:
                        wait(pe, z_ready, 4 * g - 1)
                    elif j == 1:
                        wait(pe, z_ready, 4 * g)
                    else:
                        wait(pe, xpad_filled, 6 * g + j - 1)
                    return j % 2
                if kind == "z":
                    if j < 2:
                        pe.wait_ge(xpad_filled, 6 * g + 5 + j)
                    else:
                        pe.wait_ge(z_ready, 4 * g + j - 1)
                    return j % 2
                t = 4 * it + j
                tile_n = 4 * (seg.chunk0 + it) + j
                if kind == "c":
                    if seg.start == 0 and j == 0:
                        pe.wait_ge(z_ready, 4 * GROUPS)
                    elif early:
                        pe.wait_ge(yg_ready, 4 * GROUPS)
                    else:
                        pe.wait_ge(f_ready, tile_n - 1)
                    return (3 * j) % 4
                if kind == "h":
                    if seg.start == 0 and j == 0:
                        pe.wait_ge(z_ready, 4 * GROUPS)
                    else:
                        pe.wait_ge(cmul_ready, t)
                    return (3 * j + 1) % 4
                if kind == "b":
                    if seg.start == 0 and j == 0:
                        pe.wait_ge(vsum_read, GROUPS)
                    else:
                        pe.wait_ge(prod_done, t)
                    return (3 * j + 2) % 4
                if kind in ("ga", "gb"):
                    off = 0 if kind == "ga" else 1
                    if early:
                        pe.wait_ge(f_ready, 4 * C_MIX)
                    else:
                        pe.wait_ge(sigs, 2 * (t - 2) + off + 1)
                    return (2 * j + off) % 4
                if kind == "g":
                    if early:
                        pe.wait_ge(ple_kept, 2)
                    else:
                        pe.wait_ge(spad_filled, t - 1)
                    return (2 * j) % 4
                if kind == "u":
                    if not early:
                        pe.wait_ge(f_ready, tile_n - 1)
                    return (2 * j + 1) % 4
                if kind == "pg":
                    pe.wait_ge(ple_kept, 4)
                    pe.wait_ge(sigs, 32 + 4 * it + j - 3)
                    return j

            def unit(seg, it, step, pos):
                bank = bank_free(seg, it, step)
                norm_n = {"dt": 1, "g": 2, "pg": 3}.get(step[1])
                for half in range(2):
                    slot = piece_ready(seg, it, pos + half)
                    for kk in range(8):
                        if norm_n and seg.start == 0 and step[-1] in (0, "dt") and kk % 4 == 0:
                            pe.wait_ge(n_ready, 4 * (norm_n - 1) + 2 * half + kk // 4 + 1)
                        k = 8 * half + kk
                        last = three(ps[:, bank, 0:NT], tiles(whi[slot], kk), tiles(wlo[slot], kk),
                                     n_hi[:, k, :], n_lo[:, k, :], k == 0, k == KM - 1)
                    last.then_inc(multiplied, 1)

            def rms_sum(n):
                pe.wait_ge(sq_added, ADDED[n] + (9 if n == 4 else 7))
                for t in range(2):
                    last = mm(ps[:, RMS_BANK[n], 0:NT], ones[:], sq_sum[:, t, :], start=t == 0, stop=t == 1)
                last.then_inc(sq_summed, 1)

            def rms_first():
                for h in range(4):
                    pe.wait_ge(sq_ready, h + 1)
                    for q in range(4):
                        last = mm(ps[:, RMS_BANK[1], 0:NT], ones[:], sq0[:, h % 2, q, :],
                                  start=h + q == 0, stop=h + q == 6)
                    last.then_inc(sq_summed, 1)

            def turn_inputs(j):
                if j == 3:
                    pe.wait_ge(ftab_loaded, 32)
                    for n in range(6):
                        rows = P if n < 5 else 64
                        last = turn(ps[:, 2 + n // 4, (n % 4) * P:(n % 4) * P + rows], fsrow[0:rows, n, :],
                                    ident[0:rows, 0:rows])
                        if n in (3, 5):
                            last.then_inc(ftab_turned, 1)
                if j == 4:
                    pe.wait_ge(pe_loaded, 32)
                    for kk in range(2):
                        for c in range(3):
                            rows = P if c < 2 else NS
                            last = turn(ps[:, kk, c * P:c * P + rows], perow[0:rows, c, kk * P:(kk + 1) * P],
                                        ident[0:rows, 0:rows])
                    last.then_inc(pe_turned, 1)

            def turn_tails(j):
                bank, blocks = TAIL_FOURS[j]
                if j == 0:
                    pe.wait_ge(stail_kept, 16 + DFF // P)
                if j >= 4:
                    pe.wait_ge(tail_kept, 4 * (j - 4) + 4)
                for m, rows in blocks:
                    last = turn(ps[0:rows, bank, (m % 4) * P:(m % 4) * P + P], TAIL_BLOCKS[m][1], ident[:])
                last.then_inc(tail_turned, 1)

            def head_sums(c, h, rows, width):
                return hcol[0:rows, 9 + c, h:h + 1].broadcast_to([rows, width])

            def quad(g, i):
                c, bank = QUADS[i]
                rows, n = (P, 4) if i < 4 else (NS, 8)
                mask = tri[:] if i < 4 else tri_s[:, 0:NS]
                for m in range(n):
                    h = (4 * (i % 2) if i < 4 else 0) + m
                    last = mm(ps[0:rows, bank, m * rows:(m + 1) * rows], head_sums(c, h, rows, rows), mask,
                              start=True, stop=True)
                last.then_inc(q_done, 1)

            def tasks(seg, it, step, pos):
                kind, j = step[0], step[-1]
                g = it if seg.name == "ssm" else GROUPS
                if kind == "start":
                    pe.wait_ge(x_loaded, 32)
                    pe.wait_ge(consts_ready, N_CONSTS)
                    for k in range(KM):
                        if k >= 8:
                            pe.wait_ge(x_kept_v if k % 2 else x_kept_a, (k - 8) // 2 + 1)
                        for c in range(3):
                            rows = P if c < 2 else NS
                            last = turn(ps[:, k % 8, c * P:c * P + rows], xrow[0:rows, c, k * P:(k + 1) * P],
                                        ident[0:rows, 0:rows])
                        last.then_inc(x_turned, 1)
                    pe.wait_ge(params_loaded, 16 * N_PARAM_LOADS)
                    pe.wait_ge(x_kept_v, KM // 2)
                    pe.wait_ge(x_kept_a, KM // 2)
                    for n, sources in enumerate(TAB_SOURCES):
                        for m, (src, rows) in enumerate(sources):
                            last = turn(ps[:, TAB_BANKS[n], m * P:m * P + rows], src, ident[0:rows, 0:rows])
                        last.then_inc(tab_turned, 1)
                    rms_first()
                elif kind == "unit":
                    unit(seg, it, step, pos)
                elif kind == "out":
                    pe.wait_ge(c_ready, 4 * (seg.chunk0 + it))
                    if j >= 2:
                        pe.wait_ge(out_added, 8 * (seg.chunk0 + it - 1) + j - 1)
                    slot = piece_ready(seg, it, pos)
                    if seg.name == "mixend":
                        turn_inputs(j)
                    if seg.name == "ffnend" and j < len(TAIL_FOURS):
                        turn_tails(j)
                    b0 = OUT_BANKS[j % 2]
                    for t in range(2):
                        for kk in range(4):
                            cols = slice(kk * 256 + t * P, kk * 256 + t * P + P)
                            last = three(ps[:, b0 + t, 0:NT], whi[slot][:, cols], wlo[slot][:, cols],
                                         c_hi[:, kk, :], c_lo[:, kk, :], kk == 0, kk == 3)
                    last.then_inc(multiplied, 1)
                elif kind == "ple":
                    if j == 0:
                        pe.wait_ge(pe_ready, 1)
                    if j == 0:
                        pe.wait_ge(ftab_kept, 2)
                    if j == 2:
                        pe.wait_ge(tail_kept, N_TAIL_BLOCKS)
                    if j % 2:
                        pe.wait_ge(out_added, 8 * (16 if j == 1 else 27))
                    slot = piece_ready(seg, it, pos)
                    for t in range(4):
                        if j % 2 and t == 3:
                            pe.wait_ge(var_ready, 2 + j // 2)
                        for kk in range(2):
                            cols = slice(kk * 512 + t * P, kk * 512 + t * P + P)
                            last = three(ps[:, 4 * (j % 2) + t, 0:NT], whi[slot][:, cols], wlo[slot][:, cols],
                                         peT_hi[:, kk, :], peT_lo[:, kk, :], kk == 0, kk == 1)
                    last.then_inc(multiplied, 1)
                elif kind == "rsum":
                    rms_sum(j)
                elif kind == "dtab":
                    pe.wait_ge(dt_done, 1)
                    for bank, i in ((2, 0), (3, 1)):
                        for c in range(3):
                            rows = P if c < 2 else NS
                            last = turn(ps[0:rows, bank, c * HEADS:(c + 1) * HEADS], wm[0:HEADS, i, token_rows(c)],
                                        ident[0:HEADS, 0:HEADS])
                    last.then_inc(dt_turned, 1)
                    pe.wait_ge(a_kept, 1)

                    def dta(c, rows):
                        return heads_tab[0:rows, :, 9 + c, :]
                    for bank, inner, inner_s in ((4, tri[:], tri_s[:, 0:NS]), (5, after[:], after_s[:])):
                        for c in range(2):
                            mm(ps[:, bank, c * HEADS:(c + 1) * HEADS], inner, dta(c, P), start=True, stop=True)
                        mm(ps[0:NS, bank, 2 * HEADS:3 * HEADS], inner_s, dta(2, NS), start=True, stop=True)
                    mm(ps[:, 6, 0:HEADS], after[:], dta(0, P), start=True, stop=False)
                    mm(ps[:, 6, 0:HEADS], ones[:], dta(1, P), start=False, stop=True).then_inc(dt_sums, 1)
                elif kind == "ssd1":
                    pe.wait_ge(xs_ready, 6 * g + 6)
                    wait(pe, vsum_read, g)
                    wait(pe, yg_ready, 4 * g)
                    if seg.start == 0:
                        pe.wait_ge(heads_ready, 1)
                    wait(pe, out_added, 8 * g)
                    for c in range(3):
                        rows = P if c < 2 else NS
                        for q in range(4):
                            last = turn(ps[0:rows, 2 + c, q * P:(q + 1) * P], xs[:, q, token_rows(c)], ident[:])
                        last.then_inc(xt_done, 1)
                    for c in range(3):
                        rows = P if c < 2 else NS
                        last = turn(ps[0:rows, 5, c * P:(c + 1) * P], bc[:, 0, token_rows(c)], ident[:])
                    last.then_inc(bt_done, 1)
                    for c in range(3):
                        rows = P if c < 2 else NS
                        last = mm(ps[0:rows, 6, c * P:c * P + rows], bc[:, 0, token_rows(c)], bc[:, 1, token_rows(c)],
                                  start=True, stop=True)
                    last.then_inc(cb_done, 1)
                    pe.wait_ge(hcol_ready, g + 1)
                    quad(g, 0)
                elif kind == "ssd2":
                    for i, (s, count) in enumerate(((xw_ready, 3 * g + 1), (xw_ready, 3 * g + 2),
                                                    (xw_ready, 3 * g + 3), (None, 0)), 1):
                        if s is not None:
                            pe.wait_ge(s, count)
                        if i == 3:
                            pe.wait_ge(bt_kept, g + 1)
                        quad(g, i)
                    pe.wait_ge(cbm_ready, g + 1)
                    pe.wait_ge(q_min, 5 * g + 1)
                    for half in range(2):
                        for i in range(2):
                            q = 2 * half + i
                            c0 = i * (P + NS + NB)
                            for h in range(2):
                                dst = ps[h * HD:(h + 1) * HD, 6 + half, :]
                                mm(dst[:, c0:c0 + P], head_sums(1, 2 * q + h, P, HD), tri[:], start=True, stop=True)
                                last = mm(dst[:, c0 + P:c0 + P + NS + NB], head_sums(2, 2 * q + h, NS, HD), tri_s[:],
                                          start=True, stop=True)
                        last.then_inc(ea_done, 1)
                elif kind == "ssd3":
                    pe.wait_ge(xw_ready, 3 * g + 3)
                    pe.wait_ge(bt_kept, g + 1)
                    pe.wait_ge(q_min, 5 * g + 3)
                    mm(ps[:, 2, :], bt[:, 0, :], xwe[:, 0, :], start=True, stop=True).then_inc(h1_done, 1)
                    for q in range(4):
                        cols = slice(q * P, (q + 1) * P)
                        mm(ps[:, 3, cols], xwf[:, cols], bt[:, 0, :], start=True, stop=False)
                        last = mm(ps[:, 3, cols], xwe[:, 1, cols], bt[:, 1, :], start=False, stop=True)
                    last.then_inc(h1_done, 1)
                elif kind == "pair":
                    pe.wait_ge(h0_loaded[j % 2], 16 * (2 * g + j // 2 + 1))
                    for half in range(2):
                        if j == 0:
                            pe.wait_ge(q_min, 5 * g + 5)
                        else:
                            pe.wait_ge(t_kept, 8 * g + 2 * (j - 1) + half + 1)
                        for b in range(4):
                            last = turn(ps[:, 4 + half, b * P:(b + 1) * P], h0[j % 2][:, 4 * half + b, :], ident[:])
                        last.then_inc(t_done, 1)
                    pe.wait_ge(w_ready, 5 * g + 5)
                    pe.wait_ge(ea_exp, 2 * g + 2)
                    if j:
                        pe.wait_ge(hn_added, 8 * g + 2 * j - 1)
                    for i in range(2):
                        h = 2 * j + i
                        for c in range(3):
                            rows = P if c < 2 else NS
                            quad_i = 2 * c + h // 4 if c < 2 else 4
                            m = h % 4 if c < 2 else h
                            last = mm(ps[i * HD:(i + 1) * HD, 6, token_rows(c)],
                                      xdt[0:rows, c, h * HD:(h + 1) * HD], wm[0:rows, quad_i, m * rows:(m + 1) * rows],
                                      start=True, stop=True)
                    last.then_inc(yd_done, 1)
                    pe.wait_ge(bblk_ready, g + 1)
                    pe.wait_ge(h1_kept, 2 * g + 1)
                    for half in range(2):
                        if j:
                            pe.wait_ge(hn_added, 8 * g + 2 * (j - 1) + half + 1)
                        mm(ps[:, HN_BANKS[half], :], xwe[0:NS, 2, j * P:(j + 1) * P],
                           bblk[:, 4 * half:4 * half + 4, :].rearrange("p b n -> p (b n)"),
                           start=True, stop=True).then_inc(hn_done, 1)
                    pe.wait_ge(h1_kept, 2 * g + 2)
                    pe.wait_ge(t_kept, 8 * g + 2 * j + 2)
                    if j:
                        pe.wait_ge(yg_ready, 4 * g + j)
                    mm(ps[:, 3, 0:P], h1t[:, j * P:(j + 1) * P], bc[:, 1, token_rows(1)], start=True, stop=True)
                    for b in range(NB):
                        last = mm(ps[:, 3, P + b * LB:P + (b + 1) * LB], h0t[:, b, :],
                                  bc[:, 1, SEQ + b * LB:SEQ + (b + 1) * LB], start=True, stop=True)
                    last.then_inc(yoff_done, 1)
                elif kind == "norm":
                    pe.wait_ge(ysum_ready, 3 * g)
                    pe.wait_ge(hn_added, 8 * g)
                    mm(ps[:, VS_BANK, 0:NT], ones[:], zs[:, 0, :], start=True, stop=True).then_inc(vs_done, 1)
                elif kind == "end":
                    for c in range(3):
                        rows = P if c < 2 else NS
                        for b in range(4):
                            if c == 2:
                                pe.wait_ge(y_kept_a, 1)
                                pe.wait_ge(y_kept_v, 1)
                            for m in range(4):
                                k = 4 * b + m
                                if c == 0:
                                    pe.wait_ge(y_full, b + 1)
                                last = turn(ps[0:rows, 4 * (c % 2) + b, m * P:(m + 1) * P], acc_a[:, k, token_rows(c)],
                                            ident[:])
                            last.then_inc(y_turned, 1)

            def visit(seg, it):
                pos = 0
                for step in seg.steps:
                    tasks(seg, it, step, pos)
                    pos += pieces_of(step)
            walk(pe, visit)


_INS = ["x_prompt", "x_sample", "state_ssm", "state_ssm_conv", "state_short_conv", "state_ffn_conv",
        "p_prompt", "p_sample", "norm_mix", "w_in", "ssm_conv_w", "ssm_conv_b", "ssm_dt_bias", "ssm_a_log",
        "ssm_d", "ssm_norm", "w_ssm_out", "sc_conv_w", "w_sc_out", "w_o", "norm_ffn", "w_ffn_gate", "w_ffn_up",
        "ffn_conv_w", "ffn_conv_b", "w_ffn_down", "norm_ple", "w_ple", "w_ple_gate", "norm_final"]
_OUTS = [("y_prompt", (1, SEQ, DM)), ("y_sample", (NB, LB, DM)),
         ("ssm_prompt", (1, 1, HEADS, HD, NST)), ("ssm_sample", (1, NB, HEADS, HD, NST)),
         ("xbc_prompt", (1, 1, K_X - 1, XBC)), ("xbc_sample", (1, NB, K_X - 1, XBC)),
         ("sc_prompt", (1, 1, K_SC - 1, DM)), ("sc_sample", (1, NB, K_SC - 1, DM)),
         ("ffn_prompt", (1, 1, K_F - 1, DFF)), ("ffn_sample", (1, NB, K_F - 1, DFF))]


def kernel(**inputs):
    import numpy as _np
    import concourse.bacc as _bacc
    from concourse import mybir as _mybir
    from concourse.bass_utils import run_bass_kernel_spmd as _run

    nc = _bacc.Bacc("TRN2", target_bir_lowering=False, num_devices=1, dynamic_dma_scratch_size=1024)
    arrays, ins, outs = {}, {}, {}
    for name in _INS:
        a = _np.ascontiguousarray(inputs[name])
        arrays[f"in_{name}"] = a
        ins[name] = nc.dram_tensor(f"in_{name}", a.shape, _mybir.dt.from_np(a.dtype), kind="ExternalInput").ap()
    for name, shape in _OUTS:
        outs[name] = nc.dram_tensor(f"out_{name}", shape, F32, kind="ExternalOutput").ap()
    scratch = nc.dram_tensor("residual", (P, KM, NT), F32, kind="Internal").ap()
    hybrid_decoder(nc, ins, outs, scratch)
    r = _run(nc, [arrays], core_ids=[0])
    return tuple(r.results[0][f"out_{name}"] for name, _ in _OUTS)
```
